# Optimizing a Trainium2 kernel written in Bass

```python
import math
import jax, jax.numpy as jnp
from jax import lax
import numpy as np

D_MODEL = 2048
BATCH = 1
SEQ = 256
DEPTH = 2

CHUNK = 64
Q_BLOCK = 128

FOX_HEAD_DIM = 128
FOX_HEADS = D_MODEL // (2 * FOX_HEAD_DIM)
FOX_WIDTH = FOX_HEADS * FOX_HEAD_DIM
CONV_CHANNELS = D_MODEL - FOX_WIDTH
CONV_WIDTH = 31
IN0_WIDTH = 3 * FOX_WIDTH + FOX_HEADS + 2 * CONV_CHANNELS

GDN_HEAD_DIM = 128
GDN_QK_HEADS = D_MODEL // GDN_HEAD_DIM
GDN_V_HEADS = 2 * GDN_QK_HEADS
GDN_QK_WIDTH = GDN_QK_HEADS * GDN_HEAD_DIM
GDN_V_WIDTH = GDN_V_HEADS * GDN_HEAD_DIM
GDN_QKV_WIDTH = 2 * GDN_QK_WIDTH + GDN_V_WIDTH
SHORT_CONV = 4
IN1_WIDTH = GDN_QKV_WIDTH + GDN_V_WIDTH + 2 * GDN_V_HEADS

D_FF = -(-8 * D_MODEL // (3 * 256)) * 256

N_EVEN = (DEPTH + 1) // 2
N_ODD = DEPTH // 2
NORM_EPS = 1e-6

kernel_name = "hybrid_fox_conformer_gdn_trunk"

def rms_norm(x, g):
    xf = x.astype(jnp.float32)
    y = xf * lax.rsqrt(jnp.mean(xf * xf, axis=-1, keepdims=True) + NORM_EPS)
    return (y * g.astype(jnp.float32)).astype(x.dtype)

def layer_norm(x, g, b):
    xf = x.astype(jnp.float32)
    mu = jnp.mean(xf, axis=-1, keepdims=True)
    var = jnp.mean(jnp.square(xf - mu), axis=-1, keepdims=True)
    y = (xf - mu) * lax.rsqrt(var + NORM_EPS)
    return (y * g.astype(jnp.float32) + b.astype(jnp.float32)).astype(x.dtype)

def l2_normalize(x):
    xf = x.astype(jnp.float32)
    return xf * lax.rsqrt(jnp.sum(xf * xf, axis=-1, keepdims=True) + NORM_EPS)

def causal_depthwise_conv(x, w):
    width, ch = w.shape
    return lax.conv_general_dilated(
        x, w[:, None, :].astype(x.dtype), window_strides=(1,), padding=[(width - 1, 0)],
        dimension_numbers=("NWC", "WIO", "NWC"), feature_group_count=ch)

def forgetting_attention(q, k, v, log_f):
    seq = q.shape[1]
    scale = q.shape[-1] ** -0.5
    c = jnp.transpose(jnp.cumsum(log_f, axis=1), (0, 2, 1))
    outs = []
    for blk in range(seq // Q_BLOCK):
        q0 = blk * Q_BLOCK
        kend = q0 + Q_BLOCK
        s = jnp.einsum("bqhd,bkhd->bhqk", q[:, q0:kend], k[:, :kend]).astype(jnp.float32) * scale
        s = s + c[:, :, q0:kend, None] - c[:, :, None, :kend]
        qpos = q0 + jnp.arange(Q_BLOCK)
        mask = qpos[:, None] >= jnp.arange(kend)[None, :]
        s = jnp.where(mask, s, -jnp.inf)
        p = jax.nn.softmax(s, axis=-1)
        outs.append(jnp.einsum("bhqk,bkhd->bqhd", p.astype(v.dtype), v[:, :kend]))
    return jnp.concatenate(outs, axis=1)

def fox_conformer_mixer(h, w_in, f_bias, conv_w, conv_b, ln_g, ln_b, w_out):
    bsz, seq, _ = h.shape
    proj = h @ w_in
    splits = [FOX_WIDTH, 2 * FOX_WIDTH, 3 * FOX_WIDTH, 3 * FOX_WIDTH + FOX_HEADS,
              3 * FOX_WIDTH + FOX_HEADS + CONV_CHANNELS]
    q, k, v, f_logit, glu_val, glu_gate = jnp.split(proj, splits, axis=-1)
    hs = (bsz, seq, FOX_HEADS, FOX_HEAD_DIM)
    log_f = jax.nn.log_sigmoid(f_logit.astype(jnp.float32) + f_bias.astype(jnp.float32))
    a_out = forgetting_attention(q.reshape(hs), k.reshape(hs), v.reshape(hs), log_f)
    a_out = a_out.reshape(bsz, seq, FOX_WIDTH)
    u = glu_val * jax.nn.sigmoid(glu_gate)
    u = causal_depthwise_conv(u, conv_w) + conv_b.astype(u.dtype)
    u = jax.nn.silu(layer_norm(u, ln_g, ln_b))
    return jnp.concatenate([a_out, u], axis=-1) @ w_out

def chunk_gated_delta_rule(q, k, v, g, beta):
    bsz, seq, nh, dk = q.shape
    dv = v.shape[-1]
    n = seq // CHUNK

    def to_chunks(t):
        t = t.astype(jnp.float32).reshape((bsz, n, CHUNK, nh) + t.shape[3:])
        perm = (1, 0, 3, 2) + tuple(range(4, t.ndim))
        return jnp.transpose(t, perm)

    qc, kc, vc, gc, bc = to_chunks(q), to_chunks(k), to_chunks(v), to_chunks(g), to_chunks(beta)
    gcum = jnp.cumsum(gc, axis=-1)
    idx = jnp.arange(CHUNK)
    tril = idx[:, None] >= idx[None, :]
    strict = idx[:, None] > idx[None, :]
    decay = jnp.exp(jnp.where(tril, gcum[..., :, None] - gcum[..., None, :], -jnp.inf))
    kb = kc * bc[..., None]
    vb = vc * bc[..., None]
    lower = jnp.where(strict, jnp.einsum("nbhid,nbhjd->nbhij", kb, kc) * decay, 0.0)
    a_mat = lower + jnp.eye(CHUNK, dtype=jnp.float32)
    rhs = jnp.concatenate([vb, kb * jnp.exp(gcum)[..., None]], axis=-1)
    sol = lax.linalg.triangular_solve(a_mat, rhs, left_side=True, lower=True, unit_diagonal=True)
    u_c, w_c = sol[..., :dv], sol[..., dv:]

    def step(state, inp):
        qi, ki, ui, wi, gi, di = inp
        intra = jnp.einsum("bhid,bhjd->bhij", qi, ki) * di
        v_new = ui - jnp.einsum("bhck,bhkv->bhcv", wi, state)
        o = (jnp.einsum("bhck,bhkv->bhcv", qi * jnp.exp(gi)[..., None], state)
             + jnp.einsum("bhij,bhjv->bhiv", intra, v_new))
        g_last = gi[..., -1]
        k_dec = ki * jnp.exp(g_last[..., None] - gi)[..., None]
        state = state * jnp.exp(g_last)[..., None, None] + jnp.einsum("bhck,bhcv->bhkv", k_dec, v_new)
        return state, o

    state0 = jnp.zeros((bsz, nh, dk, dv), jnp.float32)
    _, out = lax.scan(step, state0, (qc, kc, u_c, w_c, gcum, decay))
    return jnp.transpose(out, (1, 0, 3, 2, 4)).reshape(bsz, seq, nh, dv)

def gated_deltanet_mixer(h, w_in, short_conv, a_log, dt_bias, o_norm, w_out):
    bsz, seq, _ = h.shape
    proj = h @ w_in
    splits = [GDN_QKV_WIDTH, GDN_QKV_WIDTH + GDN_V_WIDTH, GDN_QKV_WIDTH + GDN_V_WIDTH + GDN_V_HEADS]
    qkv, z, b_logit, a_logit = jnp.split(proj, splits, axis=-1)
    qkv = jax.nn.silu(causal_depthwise_conv(qkv, short_conv))
    q, k, v = jnp.split(qkv, [GDN_QK_WIDTH, 2 * GDN_QK_WIDTH], axis=-1)
    rep = GDN_V_HEADS // GDN_QK_HEADS
    q = l2_normalize(q.reshape(bsz, seq, GDN_QK_HEADS, GDN_HEAD_DIM)) * (GDN_HEAD_DIM ** -0.5)
    k = l2_normalize(k.reshape(bsz, seq, GDN_QK_HEADS, GDN_HEAD_DIM))
    q = jnp.repeat(q, rep, axis=2)
    k = jnp.repeat(k, rep, axis=2)
    v = v.reshape(bsz, seq, GDN_V_HEADS, GDN_HEAD_DIM)
    beta = jax.nn.sigmoid(b_logit.astype(jnp.float32))
    g = -jnp.exp(a_log.astype(jnp.float32)) * jax.nn.softplus(
        a_logit.astype(jnp.float32) + dt_bias.astype(jnp.float32))
    o = chunk_gated_delta_rule(q, k, v, g, beta)
    zf = z.reshape(bsz, seq, GDN_V_HEADS, GDN_HEAD_DIM).astype(jnp.float32)
    o = rms_norm(o, o_norm) * jax.nn.silu(zf)
    return o.reshape(bsz, seq, GDN_V_WIDTH).astype(h.dtype) @ w_out

def swiglu_ffn(h, w_gate, w_up, w_down):
    return (jax.nn.silu(h @ w_gate) * (h @ w_up)) @ w_down

def setup_inputs(seed: int = 0) -> dict:
    key = jax.random.key(seed)
    ks = jax.random.split(key, 24)
    f32 = jnp.float32

    def nrm(k, shape, scale):
        return jax.random.normal(k, shape, f32) * scale

    def gain(k, shape):
        return 1.0 + 0.02 * jax.random.normal(k, shape, f32)

    x = nrm(ks[0], (BATCH, SEQ, D_MODEL), 1.0)
    norm_mix0 = gain(ks[1], (N_EVEN, D_MODEL))
    w_in0 = nrm(ks[2], (N_EVEN, D_MODEL, IN0_WIDTH), D_MODEL ** -0.5)
    fgate_bias0 = jnp.linspace(1.0, 5.0, FOX_HEADS, dtype=f32)[None, :] + nrm(ks[3], (N_EVEN, FOX_HEADS), 0.1)
    conv_w0 = nrm(ks[4], (N_EVEN, CONV_WIDTH, CONV_CHANNELS), CONV_WIDTH ** -0.5)
    conv_b0 = nrm(ks[5], (N_EVEN, CONV_CHANNELS), 0.02)
    conv_ln_g0 = gain(ks[6], (N_EVEN, CONV_CHANNELS))
    conv_ln_b0 = nrm(ks[7], (N_EVEN, CONV_CHANNELS), 0.02)
    w_out0 = nrm(ks[8], (N_EVEN, D_MODEL, D_MODEL), D_MODEL ** -0.5)
    norm_mix1 = gain(ks[9], (N_ODD, D_MODEL))
    w_in1 = nrm(ks[10], (N_ODD, D_MODEL, IN1_WIDTH), D_MODEL ** -0.5)
    short_conv1 = nrm(ks[11], (N_ODD, SHORT_CONV, GDN_QKV_WIDTH), SHORT_CONV ** -0.5)
    a_log1 = jnp.log(jax.random.uniform(ks[12], (N_ODD, GDN_V_HEADS), f32, 1.0, 16.0))
    dt = jnp.exp(jax.random.uniform(ks[13], (N_ODD, GDN_V_HEADS), f32, math.log(1e-3), math.log(1e-1)))
    dt_bias1 = dt + jnp.log(-jnp.expm1(-dt))
    o_norm1 = gain(ks[14], (N_ODD, GDN_HEAD_DIM))
    w_out1 = nrm(ks[15], (N_ODD, GDN_V_WIDTH, D_MODEL), GDN_V_WIDTH ** -0.5)
    norm_ffn = gain(ks[16], (DEPTH, D_MODEL))
    w_gate = nrm(ks[17], (DEPTH, D_MODEL, D_FF), D_MODEL ** -0.5)
    w_up = nrm(ks[18], (DEPTH, D_MODEL, D_FF), D_MODEL ** -0.5)
    w_down = nrm(ks[19], (DEPTH, D_FF, D_MODEL), D_FF ** -0.5)
    final_norm = gain(ks[20], (D_MODEL,))
    return {"x": x, "norm_mix0": norm_mix0, "w_in0": w_in0, "fgate_bias0": fgate_bias0,
            "conv_w0": conv_w0, "conv_b0": conv_b0, "conv_ln_g0": conv_ln_g0, "conv_ln_b0": conv_ln_b0,
            "w_out0": w_out0, "norm_mix1": norm_mix1, "w_in1": w_in1, "short_conv1": short_conv1,
            "a_log1": a_log1, "dt_bias1": dt_bias1, "o_norm1": o_norm1, "w_out1": w_out1,
            "norm_ffn": norm_ffn, "w_gate": w_gate, "w_up": w_up, "w_down": w_down,
            "final_norm": final_norm}

def reference(x, norm_mix0, w_in0, fgate_bias0, conv_w0, conv_b0, conv_ln_g0, conv_ln_b0, w_out0,
              norm_mix1, w_in1, short_conv1, a_log1, dt_bias1, o_norm1, w_out1,
              norm_ffn, w_gate, w_up, w_down, final_norm):
    h = x
    for layer in range(DEPTH):
        i = layer // 2
        if layer % 2 == 0:
            h = h + fox_conformer_mixer(rms_norm(h, norm_mix0[i]), w_in0[i], fgate_bias0[i], conv_w0[i],
                                        conv_b0[i], conv_ln_g0[i], conv_ln_b0[i], w_out0[i])
        else:
            h = h + gated_deltanet_mixer(rms_norm(h, norm_mix1[i]), w_in1[i], short_conv1[i], a_log1[i],
                                         dt_bias1[i], o_norm1[i], w_out1[i])
        h = h + swiglu_ffn(rms_norm(h, norm_ffn[layer]), w_gate[layer], w_up[layer], w_down[layer])
    return rms_norm(h, final_norm)


_drawn_inputs = setup_inputs


def setup_inputs(seed=0):
    import zlib

    import numpy as np

    out = dict(_drawn_inputs(seed))
    spreads = {}
    factors = {'norm_mix0': 3.646,
     'conv_ln_g0': 4.253,
     'conv_ln_b0': 5.274,
     'norm_mix1': 3.617,
     'o_norm1': 19.095,
     'norm_ffn': 2.831,
     'final_norm': 8.316,
     'conv_b0': 3.682}
    for name, (base, spread) in spreads.items():
        noise = np.random.default_rng([zlib.crc32(name.encode()), seed]).standard_normal(out[name].shape)
        drawn = base * np.exp(spread * noise) if base else spread * noise
        out[name] = __import__('jax').numpy.asarray(drawn.astype(out[name].dtype))
    for name, factor in factors.items():
        out[name] = (out[name] * factor).astype(out[name].dtype)
    return out
```

```python
import math
from contextlib import ExitStack

import concourse.bass as bass
from concourse import mybir

F32 = mybir.dt.float32
F32R = mybir.dt.float32r
BF16 = mybir.dt.bfloat16
ALU = mybir.AluOpType
ACT = mybir.ActivationFunctionType
AX = mybir.AxisListType

P = 128
T = 256
TT = T // P
D = 2048
KT = D // P
GW = 512
GM = GW // P
NCH = 4
EPS = 1e-6
NEG = -1e30

HEADS0 = 8
CONV_W = 31
CT = 8
F_COL = 3 * 1024
GLU_COL = F_COL + HEADS0
QK_HEADS = 16
V_HEADS = 32
SETS = 4
SQ = QK_HEADS // SETS
SV = V_HEADS // SETS
BA_COL = 12288
DFF = 5632
LEVELS = 6

G_MIX0, G_MIX1, G_FFN0, G_FFN1, G_FINAL = 0, 16, 32, 48, 64
CB, LG, LB, ON, NVEC = 80, 88, 96, 104, 105
NORM_COL = (G_MIX0, G_FFN0, G_MIX1, G_FFN1, G_FINAL)


class Group:

    def __init__(self, w, col, rhs, kind, kc=4, row=0, step=0, at=0, norm=None):
        self.w, self.col, self.rhs, self.kind = w, col, rhs, kind
        self.kc, self.row, self.step, self.at, self.norm = kc, row, step, at, norm


class Segment:

    def __init__(self, name, n, groups, early=False, ahead=False):
        self.name, self.n, self.groups = name, n, groups
        self.early = early
        self.ahead = ahead


def plan():
    def ffn(layer, norm):
        def gu(p, n):
            c = p * 2048
            return Segment(f"gu{p}", n, [
                Group(f"gate{layer}", c, "x", "gate", step=GW, norm=norm),
                Group(f"up{layer}", c, "x", "up", step=GW, at=p)], early=p == 0)

        def down(p, final=None):
            kc = 4 if p < 2 else 3
            return Segment(f"down{p}", 4, [
                Group(f"down{layer}", 0, f"h{p % 2}", "resid", kc=kc, row=p * 2048, step=GW, norm=final, at=p)])
        return [gu(0, 4), gu(1, 4), down(0), gu(2, 3), down(1), down(2, norm + 1)]

    segs = [Segment("glu", 2, [Group("in0", GLU_COL, "x", "glu_val", step=GW, norm=0),
                               Group("in0", GLU_COL + 1024, "x", "glu_gate", step=GW)], early=True),
            Segment("qkv", 2, [Group("in0", 1024 * n, "x", f"fox{n}", step=GW) for n in range(3)]),
            Segment("out0", 4, [Group("out0", 0, "h0", "resid", step=GW, norm=1)])]
    segs += ffn(0, 1)
    segs += [Segment("in1", SETS, [Group("in1", 0, "x", "gdn_q", step=GW, norm=2),
                                   Group("in1", 2048, "x", "gdn_k", step=GW),
                                   Group("in1", 4096, "x", "gdn_v0", step=2 * GW),
                                   Group("in1", 4096 + GW, "x", "gdn_v1", step=2 * GW),
                                   Group("in1", 8192, "x", "gdn_z0", step=2 * GW),
                                   Group("in1", 8192 + GW, "x", "gdn_z1", step=2 * GW)], early=True),
             Segment("out1a", 4, [Group("out1", 0, "x", "resid", step=GW)]),
             Segment("out1b", 4, [Group("out1", 0, "x", "resid", row=2048, step=GW, norm=3)])]
    segs += ffn(1, 3)
    at = resid = pair = 0
    for n, s in enumerate(segs):
        s.first = at
        at += s.n * len(s.groups)
        s.next_kc = segs[n + 1].groups[0].kc if n + 1 < len(segs) else 0
        s.ahead = n + 1 < len(segs) and segs[n + 1].early
        s.resid, s.pair = resid, pair
        if s.groups[0].kind == "resid":
            resid += s.n
        if s.groups[0].kind == "gate":
            pair += s.n
    return segs


def trunk(nc, x, norm_mix0, w_in0, fgate_bias0, conv_w0, conv_b0, conv_ln_g0, conv_ln_b0, w_out0,
          norm_mix1, w_in1, short_conv1, a_log1, dt_bias1, o_norm1, w_out1,
          norm_ffn, w_gate, w_up, w_down, final_norm, x_save, out):
    weights = {"in0": w_in0[0], "out0": w_out0[0], "in1": w_in1[0], "out1": w_out1[0]}
    for layer in range(2):
        weights[f"gate{layer}"] = w_gate[layer]
        weights[f"up{layer}"] = w_up[layer]
        weights[f"down{layer}"] = w_down[layer]
    segs = plan()
    seg_of = {}
    for n, s in enumerate(segs):
        seg_of.setdefault(s.name, []).append(s)
    n_groups = sum(s.n * len(s.groups) for s in segs)

    ctx = ExitStack()
    with ctx:
        top = [0]

        def region(size):
            at = top[0]
            top[0] += size
            return at

        def sb(name, shape, dt=F32, at=None):
            size = 2 if dt == BF16 else 4
            for s in shape[1:]:
                size *= s
            if at is None:
                at = region((size + 31) // 32 * 32)
            return nc.alloc_sbuf_tensor_at(name, shape, dt, offset=base + at)

        base = (nc.sbuf_base + 31) // 32 * 32
        raw = sb("raw", [P, NCH, 4, GW])
        w_hi = sb("w_hi", [P, 2, 4, GW], F32R)
        w_lo = sb("w_lo", [P, 2, 4, GW], F32R)
        x_at = region(KT * 2 * T * 4)
        xs = sb("xs", [P, KT, 2, T], F32R, at=x_at)
        h_at = region(2 * KT * 2 * T * 4)
        hs = [sb(f"hs{p}", [P, KT, 2, T], F32R, at=h_at + p * 32768) for p in range(2)]
        r_at = region(KT * T * 4)
        xT = sb("xT", [P, KT, T], at=r_at)
        xn_at = region(8192)
        xn = sb("xn", [P, 2, 4, T], at=xn_at)
        ut = sb("ut", [P, GM, T])
        gt = sb("gt", [P, GM, T])
        tmp = sb("tmp", [P, 2, T])
        sq_acc = sb("sq_acc", [P, T])
        sq_one = sb("sq_one", [P, T])
        rms = sb("rms", [P, T])
        rstd = sb("rstd", [P, T])
        ident = sb("ident", [P, P])
        ones = sb("ones", [P, P])
        triu = sb("triu", [P, P])
        chunk_triu = sb("chunk_triu", [P, P])
        chunk_ones = sb("chunk_ones", [P, P])
        mask_fox = sb("mask_fox", [P, P])
        mask_gdn = sb("mask_gdn", [P, P])
        lvl = sb("lvl", [P, LEVELS, P], BF16)
        lvl0t = sb("lvl0t", [P, P], BF16)
        vec = sb("vec", [P, NVEC])
        conv_w = sb("conv_w", [P, CONV_W, CT])
        short_w = sb("short_w", [P, 4, 64])
        bias = sb("bias", [P, 72])
        eps = sb("eps", [P, 4])
        small = sb("small", [P, 2, 64])

        h1 = h_at + 32768
        qT = sb("qT", [P, HEADS0, T], at=h1)
        kT = sb("kT", [P, HEADS0, T], at=h1 + 8192)
        vT = sb("vT", [P, HEADS0, T], at=h1 + 16384)
        ncT = sb("ncT", [HEADS0, T], at=h1 + 24576)
        logf = sb("logf", [P, TT, HEADS0], at=h1 + 25600)
        cq = sb("cq", [P, TT, HEADS0], at=h1 + 25664)
        mx = sb("mx", [P, 2, TT], at=h1 + 25728)
        rsum = sb("rsum", [P, 2, TT], at=h1 + 25760)
        rinv = sb("rinv", [P, 2, TT], at=h1 + 25792)
        sp = [sb(f"sp{n}", [P, 64], at=h1 + 26624 + 256 * n) for n in range(8)]
        u_pad = sb("u_pad", [P, CT, CONV_W - 1 + T], at=h_at)
        u_sq = sb("u_sq", [P, CT, T], at=h_at)
        conv = sb("conv", [P, CT, T], at=xn_at)
        v_tok = sb("v_tok", [P, HEADS0, TT, P], at=x_at)
        sc = sb("sc", [P, 2, 2, T], at=x_at + 8192)
        pT = sb("pT", [P, 2, 384], at=x_at + 12288)
        stage = sb("stage", [P, TT, D], at=h1)
        vrow = sb("vrow", [P, 5, P], at=h_at)
        brow = sb("brow", [1, 72], at=h_at + 4096)
        wsm = sb("wsm", [P, KT, 64], at=h_at + 16384)
        wsm_s = sb("wsm_s", [P, KT, P], F32R, at=h_at + 8192 + 16384)

        og = sb("og", [P, V_HEADS, T], at=h_at)
        qk = sb("qk", [P, 2, SQ, T], at=h_at + 32768)
        vs = sb("vs", [P, SV, T], at=h_at + 40960)
        zs = sb("zs", [P, SV, T], at=h_at + 49152)
        slot_at = [r_at + 2048 * n for n in range(8)] + [xn_at + 2048 * n for n in range(4)] \
            + [h_at + 57344 + 2048 * n for n in range(4)]
        slot = [[sb(f"slot{p}_{n}", [P, 4, P], at=slot_at[7 * p + n]) for n in range(7)] for p in range(2)]
        state = [sb(f"state{p}", [P, 2, P], at=slot_at[14] + 1024 * p) for p in range(2)]
        qk_sq = sb("qk_sq", [P, 2, SQ, T], at=r_at)
        gate_b = sb("gate_b", [P, TT, V_HEADS])
        gate_g = sb("gate_g", [P, TT, V_HEADS])
        gate_c = sb("gate_c", [P, TT, V_HEADS])
        gate_ec = sb("gate_ec", [P, TT, V_HEADS], at=h_at + 63488)
        gate_ed = sb("gate_ed", [P, TT, V_HEADS], at=h_at + 63744)
        gate_bg = sb("gate_bg", [P, TT, V_HEADS], at=h_at + 64000)
        gate_el = sb("gate_el", [P, 2 * TT, V_HEADS], at=h_at + 64256)
        g_set = sb("g_set", [P, TT, SV])
        o_ss = sb("o_ss", [P, 2, 4])
        o_rs = sb("o_rs", [P, 2, 4])
        assert top[0] <= 212800, top[0]
        ctx.enter_context(nc.sbuf_tensor("arena", [P, top[0] // 4], F32))

        acc = ctx.enter_context(nc.psum_tensor("acc", [P, GM, GW], F32))
        aux = [ctx.enter_context(nc.psum_tensor(f"aux{n}", [P, 512], F32)) for n in range(4)]

        def sem(name):
            return ctx.enter_context(nc.semaphore(name))

        raw_in = [sem(f"raw_in{n}") for n in range(NCH)]
        hi_ready, lo_ready, w_used = sem("hi_ready"), sem("lo_ready"), sem("w_used")
        acc_ready, tmp_ready, acc_free = sem("acc_ready"), sem("tmp_ready"), sem("acc_free")
        const_in, x_in, const_step, const_pe, const_cp = (sem(n) for n in
            ("const_in", "x_in", "const_step", "const_pe", "const_cp"))
        x_trans, x_copied = sem("x_trans"), sem("x_copied")
        resid_added, sq_made, sq_added = sem("resid_added"), sem("sq_made"), sem("sq_added")
        ss_ready, rms_ready, rstd_ready = sem("ss_ready"), sem("rms_ready"), sem("rstd_ready")
        xn_ready, xsh_ready, xs_ready = sem("xn_ready"), sem("xsh_ready"), sem("xs_ready")
        gate_silu, h_prod, h_hi, h_ready = sem("gate_silu"), sem("h_prod"), sem("h_hi"), sem("h_ready")
        wsm_in, wsm_hi, wsm_lo, wsm_mm = sem("wsm_in"), sem("wsm_hi"), sem("wsm_lo"), sem("wsm_mm")
        sp_dve, sp_act = sem("sp_dve"), sem("sp_act")
        fox_pe0, fox_cp = sem("fox_pe0"), sem("fox_cp")
        glu_sig, glu_made, conv_step = sem("glu_sig"), sem("glu_made"), sem("conv_step")
        ln_pe, ln_dve, ln_act = sem("ln_pe"), sem("ln_dve"), sem("ln_act")
        vt_pe, vt_act = sem("vt_pe"), sem("vt_act")
        fx_pe = [sem(f"fx_pe{p}") for p in range(2)]
        fx_dve = [sem(f"fx_dve{p}") for p in range(2)]
        fx_act = [sem(f"fx_act{p}") for p in range(2)]
        fx_pool = [sem(f"fx_pool{p}") for p in range(2)]
        gg_pe, gg_dve, gg_act = sem("gg_pe"), sem("gg_dve"), sem("gg_act")
        sc_step, conv_silu = sem("sc_step"), sem("conv_silu")
        l2_act, l2_pe, l2_dve, gset_ready = sem("l2_act"), sem("l2_pe"), sem("l2_dve"), sem("gset_ready")
        gd_pe = [sem(f"gd_pe{p}") for p in range(2)]
        gd_dve = [sem(f"gd_dve{p}") for p in range(2)]
        gd_act = [sem(f"gd_act{p}") for p in range(2)]
        gd_pool = [sem(f"gd_pool{p}") for p in range(2)]
        pool_mark = sem("pool_mark")
        fg_tmp, fox_lf = sem("fg_tmp"), sem("fox_lf")
        x_saved, x_back = sem("x_saved"), sem("x_back")
        og_hi, og_ready = sem("og_hi"), sem("og_ready")
        y_made, y_pe, y_out, out_sent = sem("y_made"), sem("y_pe"), sem("y_out"), sem("out_sent")


        def rhs_of(g):
            return {"x": xs, "h0": hs[0], "h1": hs[1]}[g.rhs]

        def rounds(eng, s, body, peel_first=False, peel_last=False):
            lo, hi = int(peel_first), s.n - int(peel_last)
            if peel_first:
                body(0, s.n == 1)
            if hi > lo:
                if hi - lo == 1:
                    body(lo, lo == s.n - 1)
                else:
                    with eng.Fori(lo, hi) as i:
                        body(i, False)
            if peel_last and s.n > lo:
                body(s.n - 1, True)

        def apart(pool):
            pool.sem_inc(pool_mark, 1)

        def number(s, i, b):
            return s.first + len(s.groups) * i + b

        def sync_program(sp_e):
            sp_e.dma_start(stage[:], x.rearrange("o (t p) d -> p (o t) d", p=P)).then_inc(x_in, 16)

            def load(s, i, b, g):
                w = weights[g.w]
                for c in range(NCH):
                    G = number(s, i, b)
                    if not (isinstance(G, int) and G == 0):
                        sp_e.wait_ge(lo_ready, 4 * G + c - 3)
                    r0 = g.row + c * g.kc * P
                    col = bass.ds(g.col + g.step * i, GW)
                    sp_e.dma_start(raw[:, c, 0:g.kc], w[r0:r0 + g.kc * P, col].rearrange("(k p) n -> p k n", p=P))\
                        .then_inc(raw_in[c], 16)

            for s in segs:
                def body(i, last, s=s):
                    for b, g in enumerate(s.groups):
                        load(s, i, b, g)
                rounds(sp_e, s, body, peel_first=s.first == 0)
            for t in range(TT):
                sp_e.wait_ge(y_out, 15 + t)
                sp_e.dma_start(out[0, t * P:(t + 1) * P, :], stage[:, t]).then_inc(out_sent, 16)
            sp_e.wait_ge(out_sent, 16 * TT)

        def pool_program(pool):
            steps = [0]

            def link(ins):
                steps[0] += 1
                ins.then_inc(const_step, 1)
                pool.wait_ge(const_step, steps[0])

            rows = [(norm_mix0, G_MIX0, 16), (norm_mix1, G_MIX1, 16), (norm_ffn, G_FFN0, 32),
                    (final_norm, G_FINAL, 16), (conv_b0, CB, 8), (conv_ln_g0, LG, 8), (conv_ln_b0, LB, 8),
                    (o_norm1, ON, 1)]
            for src, r, n in rows:
                flat = src if len(src.shape) == 1 else src.rearrange("a b -> (a b)")
                pool.dma_start(vrow[r:r + n, 0, :], flat.rearrange("(a b) -> a b", b=P)).then_inc(const_in, 16)
            cw = conv_w0[0].rearrange("w (c p) -> (w c) p", p=P)
            pool.dma_start(vrow[0:124, 1, :], cw[0:124]).then_inc(const_in, 16)
            pool.dma_start(vrow[0:124, 2, :], cw[124:248]).then_inc(const_in, 16)
            sw = short_conv1[0].rearrange("w (c p) -> (w c) p", p=P)
            pool.dma_start(vrow[:, 3, :], sw[0:128]).then_inc(const_in, 16)
            pool.dma_start(vrow[:, 4, :], sw[128:256]).then_inc(const_in, 16)
            pool.dma_start(brow[:, 0:8], fgate_bias0).then_inc(const_in, 16)
            pool.dma_start(brow[:, 8:40], a_log1).then_inc(const_in, 16)
            pool.dma_start(brow[:, 40:72], dt_bias1).then_inc(const_in, 16)
            pool.dma_start(wsm[:, :, 0:HEADS0], w_in0[0, :, F_COL:F_COL + HEADS0]
                           .rearrange("(k p) n -> p k n", p=P)).then_inc(wsm_in, 16)

            def select(m, pattern, base_, mult, fill=0.0, op=ALU.is_ge):
                link(pool.affine_select(out=m, in_=m, compare_op=op, fill=fill, base=base_,
                                        pattern=pattern, channel_multiplier=mult))

            link(pool.memset(ident[:], 0.0))
            select(ident[:], [[-1, P]], 0, 1, fill=1.0, op=ALU.not_equal)
            link(pool.memset(ones[:], 1.0))
            link(pool.memset(triu[:], 1.0))
            select(triu[:], [[1, P]], 0, -1)
            link(pool.memset(chunk_triu[:], 1.0))
            select(chunk_triu[:], [[1, P]], 0, -1)
            select(chunk_triu[:, 64:P], [[0, 64]], -64, 1)
            link(pool.memset(chunk_ones[:], 1.0))
            select(chunk_ones[:, 64:P], [[0, 64]], -64, 1)
            select(chunk_ones[:, 0:64], [[0, 64]], 63, -1)
            link(pool.memset(mask_fox[:], 0.0))
            select(mask_fox[:], [[-1, P]], 0, 1, fill=NEG)
            link(pool.memset(mask_gdn[:], 0.0))
            select(mask_gdn[:], [[-1, P]], 0, 1, fill=NEG)
            select(mask_gdn[:, 0:64], [[0, 64]], 63, -1, fill=NEG)
            link(pool.memset(lvl[:], 0.0))
            for n in range(LEVELS):
                s = 1 << n
                upper = lvl[:, n, :].rearrange("p (b h w) -> p b h w", h=2, w=s)[:, :, 1, :]
                link(pool.memset(upper, 1.0))
                select(upper, [[-2 * s, P // (2 * s)], [0, s]], 0, 1)
                select(upper, [[2 * s, P // (2 * s)], [0, s]], s - 1, -1)
            link(pool.memset(lvl0t[:], 0.0))
            lower = lvl0t[:, :].rearrange("p (b h) -> p b h", h=2)[:, :, 0]
            link(pool.memset(lower, 1.0))
            select(lower, [[-2, P // 2]], -1, 1, fill=0.0, op=ALU.is_equal)
            for n, v in enumerate((EPS, P * EPS)):
                link(pool.memset(eps[:, n:n + 1], v))
            assert steps[0] == N_CONST, steps[0]
            pool.wait_ge(const_pe, 6)
            link(pool.memset(u_pad[:, :, 0:CONV_W - 1], 0.0))

            def squares(n, count, tile):
                pool.wait_ge(sq_added, 16 * n + count)
                apart(pool)
                nc.gpsimd.tensor_tensor(sq_one[:], tile, tile, ALU.mult).then_inc(sq_made, 1)
                pool.wait_ge(sq_made, 16 * n + count + 1)
                nc.gpsimd.tensor_tensor(sq_acc[:], sq_acc[:], sq_one[:], ALU.add).then_inc(sq_added, 1)

            link(pool.memset(sq_acc[:], 0.0))
            for k in range(KT):
                pool.wait_ge(x_copied, k + 1)
                pool.wait_ge(sq_added, k) if k else None
                nc.gpsimd.tensor_tensor(sq_one[:], xT[:, k], xT[:, k], ALU.mult).then_inc(sq_made, 1)
                pool.wait_ge(sq_made, k + 1)
                nc.gpsimd.tensor_tensor(sq_acc[:], sq_acc[:], sq_one[:], ALU.add).then_inc(sq_added, 1)

            for s in segs:
                if s.name == "out0":
                    fox_pool(pool)
                if s.name == "in1":
                    pool.wait_ge(h_ready, s.pair)
                    pool.wait_ge(ss_ready, 3)
                    pool.wait_ge(acc_ready, 4 * s.first)
                    pool.dma_start(wsm[:], w_in1[0, :, BA_COL:BA_COL + 64]
                                   .rearrange("(k p) n -> p k n", p=P)).then_inc(wsm_in, 16)
                if s.groups[0].norm is not None and s.groups[0].kind == "resid":
                    pool.wait_ge(ss_ready, s.groups[0].norm)
                    link(pool.memset(sq_acc[:], 0.0))

                def body(i, last, s=s):
                    for b, g in enumerate(s.groups):
                        G = number(s, i, b)
                        if g.kind == "resid":
                            for m in range(GM):
                                pool.wait_ge(acc_free, 4 * G + m + 1)
                                apart(pool)
                                row = xT[:, bass.ds(4 * i + m, 1), :].rearrange("p a t -> p (a t)")
                                nc.gpsimd.tensor_tensor(row, row, ut[:, m], ALU.add).then_inc(resid_added, 1)
                                if g.norm is not None:
                                    pool.wait_ge(resid_added, 4 * (s.resid + i) + m + 1)
                                    squares(g.norm, 4 * i + m, row)
                        if g.kind == "glu_gate":
                            pool.wait_ge(glu_sig, i + 1)
                            apart(pool)
                            nc.gpsimd.tensor_tensor(u_pad[:, bass.ds(4 * i, 4), CONV_W - 1:], gt[:], ut[:],
                                                    ALU.mult).then_inc(glu_made, 1)
                        if g.kind == "up":
                            q = s.pair + i
                            pool.wait_ge(gate_silu, q + 1)
                            pool.wait_ge(acc_free, 4 * G + 4)
                            nc.gpsimd.tensor_tensor(ut[:], gt[:], ut[:], ALU.mult).then_inc(h_prod, 1)
                            pool.wait_ge(h_prod, q + 1)
                            apart(pool)
                            hb = hs[g.at % 2]
                            hi = hb[:, bass.ds(4 * i, 4), 0, :]
                            nc.gpsimd.tensor_copy(hi, ut[:]).then_inc(h_hi, 1)
                            pool.wait_ge(h_hi, q + 1)
                            apart(pool)
                            nc.gpsimd.tensor_tensor(hb[:, bass.ds(4 * i, 4), 1, :], ut[:], hi.bitcast(F32),
                                                    ALU.subtract).then_inc(h_ready, 1)
                        if g.kind == "gdn_z1":
                            gdn_pool(pool, i)
                if s.name == "out1a":
                    pool.wait_ge(x_back, 16)
                rounds(pool, s, body)

        def scalar_program(act):
            def split_hi(G, c, kc):
                act.wait_ge(raw_in[c], 16 * G + 16)
                if not (isinstance(G, int) and G == 0 and c < 2):
                    if c == 1:
                        act.wait_ge(acc_ready, 4 * G)
                    else:
                        act.wait_ge(w_used, 3 * G + (c - 1 if c else 0))
                nc.scalar.activation(w_hi[:, c % 2, 0:kc], raw[:, c, 0:kc], ACT.Copy).then_inc(hi_ready, 1)

            def sums(G, g):
                for m in range(GM):
                    act.wait_ge(acc_ready, 4 * G + m + 1)
                    if not (isinstance(G, int) and G == 0 and m < 2):
                        act.wait_ge(acc_free, 4 * G + m - 1)
                    nc.scalar.activation(tmp[:, m % 2], acc[:, m, T:2 * T], ACT.Copy).then_inc(tmp_ready, 1)

            act.wait_ge(const_step, N_CONST)
            act.wait_ge(const_pe, 6)
            nc.scalar.activation(vec[:], aux[0][:, 0:NVEC], ACT.Copy).then_inc(const_cp, 1)
            nc.scalar.activation(conv_w[:].rearrange("p w c -> p (w c)"), aux[1][:, 0:248], ACT.Copy).then_inc(const_cp, 1)
            nc.scalar.activation(short_w[:].rearrange("p w c -> p (w c)"), aux[2][:, 0:256], ACT.Copy).then_inc(const_cp, 1)
            nc.scalar.activation(bias[:], aux[3][:, 0:72], ACT.Copy).then_inc(const_cp, 1)
            for k in range(0, KT, 2):
                act.wait_ge(x_trans, k // 2 + 1)
                for h in range(2):
                    nc.scalar.activation(xT[:, k + h], acc[:, (k // 2) % 4, h * T:(h + 1) * T], ACT.Copy)\
                        .then_inc(x_copied, 1)
            split_hi(0, 0, 4)
            split_hi(0, 1, 4)
            for s in segs:
                g0 = s.groups[0]
                if s.early:
                    norm_act(act, g0.norm)
                if s.name == "glu":
                    small_act(act, 0, HEADS0)
                    softplus_act(act, 0)
                    fox_gate_act(act)
                if s.name == "out0":
                    ln_act_steps(act)
                    fox_act(act)
                if s.name == "in1":
                    act.dma_start(x_save.rearrange("(k p) t -> p k t", p=P), xT[:]).then_inc(x_saved, 16)
                    small_act(act, 1, 64)
                    gates_act(act)
                if s.name in ("out1a", "out1b"):
                    n = int(s.name == "out1b")
                    for p in range(2):
                        act.wait_ge(gd_dve[p], ND * 2 * SETS)
                        act.wait_ge(gd_pe[p], NP * 2 * SETS)
                    if n == 0:
                        act.dma_start(xT[:], x_save.rearrange("(k p) t -> p k t", p=P)).then_inc(x_back, 16)
                    act.wait_ge(acc_ready, 4 * s.first)
                    for c in range(4):
                        nc.scalar.activation(xs[:, 4 * c:4 * c + 4, 0, :], og[:, 16 * n + 4 * c:16 * n + 4 * c + 4],
                                             ACT.Copy).then_inc(og_hi, 1)

                def body(i, last, s=s):
                    for b, g in enumerate(s.groups):
                        G = number(s, i, b)
                        done = 2 if s.early and isinstance(i, int) and i == 0 and b == 0 else 1
                        for c in range(done, NCH):
                            split_hi(G, c, g.kc)
                        end = last and b == len(s.groups) - 1
                        kc = s.next_kc if end else s.groups[(b + 1) % len(s.groups)].kc
                        if kc:
                            split_hi(G + 1, 0, kc)
                        sums(G, g)
                        if end and s.ahead:
                            split_hi(G + 1, 1, kc)
                        if g.kind == "gate":
                            act.wait_ge(acc_free, 4 * G + 4)
                            nc.scalar.activation(gt[:], gt[:], ACT.Silu).then_inc(gate_silu, 1)
                        if g.kind == "glu_gate":
                            act.wait_ge(acc_free, 4 * G + 4)
                            nc.scalar.activation(gt[:], gt[:], ACT.Sigmoid).then_inc(glu_sig, 1)
                        if g.kind.startswith("gdn"):
                            if b < 4:
                                act.wait_ge(sc_step, 4 * (4 * i + b) + 4)
                            else:
                                act.wait_ge(acc_free, 4 * G + 4)
                            dst = {"gdn_q": qk[:, 0], "gdn_k": qk[:, 1], "gdn_v0": vs[:, 0:4], "gdn_v1": vs[:, 4:8],
                                   "gdn_z0": zs[:, 0:4], "gdn_z1": zs[:, 4:8]}[g.kind]
                            nc.scalar.activation(dst, gt[:], ACT.Silu).then_inc(conv_silu, 1)
                        if g.kind == "gdn_z1":
                            gdn_act(act, i)
                rounds(act, s, body, peel_first=s.early, peel_last=peel_last(s))
            norm_act(act, 4, split=False)
            for k in range(KT // 2):
                act.wait_ge(y_pe, k + 1)
                for t in range(TT):
                    nc.scalar.activation(stage[:, t, k * T:(k + 1) * T], aux[(2 * k + t) % 4][:, 0:T], ACT.Copy)\
                        .then_inc(y_out, 1)


        def peel_last(s):
            return s.groups[0].kc != s.next_kc or s.ahead

        def norm_act(act, n, split=True):
            act.wait_ge(ss_ready, n + 1)
            nc.scalar.activation(rms[:], aux[0][:, 0:T], ACT.Sqrt, bias=eps[:, 0:1], scale=1.0 / D).then_inc(rms_ready, 1)
            if split:
                for c in range(4):
                    act.wait_ge(xn_ready, 4 * n_xn(n) + c + 1)
                    nc.scalar.activation(xs[:, 4 * c:4 * c + 4, 0, :], xn[:, c % 2], ACT.Copy).then_inc(xsh_ready, 1)

        def n_xn(n):
            return n

        def small_act(act, which, n):
            act.wait_ge(wsm_in, 16 * (which + 1))
            nc.scalar.activation(wsm_s[:, :, 0:n], wsm[:, :, 0:n], ACT.Copy).then_inc(wsm_hi, 1)

        def softplus_act(act, n):
            act.wait_ge(sp_dve, SPD * n + 3)
            nc.scalar.activation(sp[2][:], sp[1][:], ACT.Exp, scale=-1.0).then_inc(sp_act, 1)
            act.wait_ge(sp_dve, SPD * n + 4)
            nc.scalar.activation(sp[4][:], sp[3][:], ACT.Ln).then_inc(sp_act, 1)

        def fox_gate_act(act):
            act.wait_ge(fox_pe0, 1)
            nc.scalar.activation(ncT[:], aux[1][0:HEADS0, 0:T], ACT.Copy, scale=-math.sqrt(P)).then_inc(fox_cp, 1)
            nc.scalar.activation(cq[:].rearrange("p t h -> p (t h)"), aux[2][:, 0:16], ACT.Copy).then_inc(fox_cp, 1)

        def ln_act_steps(act):
            act.wait_ge(ln_dve, 1)
            nc.scalar.activation(u_sq[:], conv[:], ACT.Square).then_inc(ln_act, 1)
            act.wait_ge(ln_pe, 2)
            nc.scalar.activation(rms[:], aux[1][:, 0:T], ACT.Sqrt, bias=eps[:, 0:1], scale=1.0 / 1024).then_inc(ln_act, 1)
            act.wait_ge(ln_dve, 3)
            for c in range(CT):
                last = nc.scalar.activation(u_sq[:, c], conv[:, c], ACT.Silu, scale=vec[:, LG + c:LG + c + 1],
                                            bias=vec[:, LB + c:LB + c + 1])
            last.then_inc(ln_act, 1)
            act.wait_ge(ln_act, 3)
            nc.scalar.activation(hs[0][:, 8:16, 0, :], u_sq[:], ACT.Copy).then_inc(ln_act, 1)

        def fox_act(act):
            for h in range(HEADS0):
                act.wait_ge(vt_pe, h + 1)
                nc.scalar.activation(v_tok[:, h], aux[h % 2][:, 0:T], ACT.Copy).then_inc(vt_act, 1)
            for h in range(HEADS0):
                p, n = h % 2, h // 2
                act.wait_ge(fx_dve[p], 5 * n + 2)
                act.wait_ge(fx_pool[p], n + 1)
                act.wait_ge(fx_dve[p], 5 * n + 2)
                for t in range(TT):
                    w = sc[:, p, t, 0:P * (t + 1)]
                    last = nc.scalar.activation(w, w, ACT.Exp, bias=mx[:, p, t:t + 1], accum_out=rsum[:, p, t:t + 1])
                    last.then_inc(fx_act[p], 1)
                act.wait_ge(fx_pe[p], 3 * n + 2)
                nc.scalar.activation(pT[:, p], aux[2 * p + 1][:, 0:384], ACT.Copy).then_inc(fx_act[p], 1)
                act.wait_ge(fx_pe[p], 3 * n + 3)
                act.wait_ge(ln_dve, 4)
                nc.scalar.activation(hs[0][:, h, 0, :], aux[2 * p][:, 0:T], ACT.Copy).then_inc(fx_act[p], 1)

        def gates_act(act):
            act.wait_ge(gg_dve, 1)
            nc.scalar.activation(gate_b[:], small[:, :, 0:32], ACT.Sigmoid).then_inc(gg_act, 1)
            softplus_act(act, 1)
            act.wait_ge(gg_act, 1)
            nc.scalar.activation(small[:, 0, 0:32], bias[:, 8:40], ACT.Exp).then_inc(gg_act, 1)
            act.wait_ge(gg_pe, 1)
            nc.scalar.activation(gate_c[:].rearrange("p t h -> p (t h)"), aux[1][:, 0:64], ACT.Copy).then_inc(gg_act, 1)
            nc.scalar.activation(gate_ec[:].rearrange("p t h -> p (t h)"), aux[1][:, 0:64], ACT.Exp).then_inc(gg_act, 1)
            act.wait_ge(gg_pe, 2)
            nc.scalar.activation(gate_el[:].rearrange("p c h -> p (c h)"), aux[3][:, 0:128], ACT.Exp).then_inc(gg_act, 1)
            act.wait_ge(gg_dve, 4)
            nc.scalar.activation(gate_ed[:], gate_ed[:], ACT.Exp).then_inc(gg_act, 1)

        def gdn_act(act, j):
            act.wait_ge(conv_silu, 6 * j + 6)
            act.wait_ge(x_saved, 16)
            if not (isinstance(j, int) and j == 0):
                for p in range(2):
                    act.wait_ge(gd_dve[p], ND * 2 * j)
            nc.scalar.activation(qk_sq[:], qk[:], ACT.Square).then_inc(l2_act, 1)
            act.wait_ge(l2_pe, j + 1)
            for n in range(4):
                q = n < 2
                nc.scalar.activation(qk_sq[:, n // 2, 2 * (n % 2):2 * (n % 2) + 2, :].rearrange("p a t -> p (a t)"),
                                     aux[n][:], ACT.Sqrt, bias=eps[:, 1:2] if q else eps[:, 0:1],
                                     scale=float(P) if q else 1.0).then_inc(l2_act, 1)
            for u in range(2):
                for step in gdn_act_steps(act, j, u):
                    pass

        def flat(t):
            return t.rearrange("p a b -> p (a b)")

        def gdn_act_steps(act, j, u):
            n = 2 * j + u
            for p in range(2):
                s0 = slot[p][0]
                act.wait_ge(gd_pool[p], NO * n + O_MASK)
                nc.scalar.activation(s0[:], s0[:], ACT.Exp).then_inc(gd_act[p], 1)
            for p in range(2):
                act.wait_ge(gd_pe[p], NP * n + P_LT)
                nc.scalar.activation(flat(slot[p][4][:]), aux[2 * p][:], ACT.Copy).then_inc(gd_act[p], 1)
                act.wait_ge(gd_pe[p], NP * n + P_IT)
                nc.scalar.activation(flat(slot[p][3][:]), aux[2 * p + 1][:], ACT.Copy).then_inc(gd_act[p], 1)
            for lv in range(1, LEVELS):
                for p in range(2):
                    act.wait_ge(gd_pe[p], NP * n + P_LV(lv, 0))
                    nc.scalar.activation(flat(slot[p][2][:]), aux[2 * p][:], ACT.Copy).then_inc(gd_act[p], 1)
                if lv < LEVELS - 1:
                    for p in range(2):
                        act.wait_ge(gd_pe[p], NP * n + P_LV(lv, 2))
                        nc.scalar.activation(flat(slot[p][6][:]), aux[2 * p][:], ACT.Copy).then_inc(gd_act[p], 1)
            for p in range(2):
                act.wait_ge(gd_pe[p], NP * n + P_U)
                nc.scalar.activation(flat(slot[p][4][:]), aux[2 * p][:], ACT.Copy).then_inc(gd_act[p], 1)
                act.wait_ge(gd_pe[p], NP * n + P_W)
                nc.scalar.activation(flat(slot[p][5][:]), aux[2 * p + 1][:], ACT.Copy).then_inc(gd_act[p], 1)
            for c in range(1, 4):
                t, r = c // 2, slice(64 * (c % 2), 64 * (c % 2) + 64)
                for p in range(2):
                    a = 2 * u + p
                    act.wait_ge(gd_dve[p], ND * n + D_VN(c))
                    for b in range(2):
                        nc.scalar.activation(slot[p][1][r, 2 * b + t, :], aux[2 * p][r, (2 + b) * P:(3 + b) * P], ACT.Copy,
                                             scale=gate_ec[r, t, bass.ds(SV * j + 2 * a + b, 1)]).then_inc(gd_act[p], 1)
            for p in range(2):
                act.wait_ge(gd_dve[p], ND * n + D_SS)
                nc.scalar.activation(o_rs[:, p], o_ss[:, p], ACT.Sqrt, bias=eps[:, 0:1], scale=1.0 / P)\
                    .then_inc(gd_act[p], 1)
            yield

        def vector_program(dve):
            def split_lo(G, c, kc):
                dve.wait_ge(hi_ready, 4 * G + c + 1)
                nc.vector.tensor_tensor(w_lo[:, c % 2, 0:kc], raw[:, c, 0:kc], w_hi[:, c % 2, 0:kc].bitcast(F32),
                                        ALU.subtract).then_inc(lo_ready, 1)

            def sums(G, dst):
                for m in range(GM):
                    dve.wait_ge(tmp_ready, 4 * G + m + 1)
                    nc.vector.tensor_tensor(dst(m), acc[:, m, 0:T], tmp[:, m % 2], ALU.add).then_inc(acc_free, 1)

            dve.wait_ge(const_step, N_CONST)
            split_lo(0, 0, 4)
            split_lo(0, 1, 4)
            for s in segs:
                g0 = s.groups[0]
                if s.early:
                    norm_dve(dve, g0.norm)
                if s.name == "glu":
                    small_dve(dve, 0, HEADS0)
                    fox_gate_dve(dve)
                if s.name == "qkv":
                    dve.wait_ge(glu_made, 2)
                    for c in range(CT):
                        nc.vector.tensor_scalar(conv[:, c], u_pad[:, c, 0:T], conv_w[:, 0, c:c + 1],
                                                vec[:, CB + c:CB + c + 1], ALU.mult, ALU.add).then_inc(conv_step, 1)
                if s.name == "out0":
                    ln_dve_steps(dve)
                    fox_dve(dve)
                if s.name == "in1":
                    small_dve(dve, 1, 64)
                    gates_dve(dve)
                if s.name in ("out1a", "out1b"):
                    n = int(s.name == "out1b")
                    for c in range(4):
                        dve.wait_ge(og_hi, 4 * n + c + 1)
                        nc.vector.tensor_tensor(xs[:, 4 * c:4 * c + 4, 1, :], og[:, 16 * n + 4 * c:16 * n + 4 * c + 4],
                                                xs[:, 4 * c:4 * c + 4, 0, :].bitcast(F32), ALU.subtract)\
                            .then_inc(og_ready, 1)

                def body(i, last, s=s):
                    for b, g in enumerate(s.groups):
                        G = number(s, i, b)
                        done = 2 if s.early and isinstance(i, int) and i == 0 and b == 0 else 1
                        end = last and b == len(s.groups) - 1
                        kc = s.next_kc if end else s.groups[(b + 1) % len(s.groups)].kc
                        for c in range(done, NCH):
                            split_lo(G, c, g.kc)
                            if s.name == "qkv":
                                conv_taps(dve, i, 4 * b + c - 1)
                        if kc:
                            split_lo(G + 1, 0, kc)
                        if s.name == "qkv":
                            conv_taps(dve, i, 4 * b + 3)
                        if g.kind == "resid":
                            if not (s.resid == 0 and isinstance(i, int) and i == 0):
                                dve.wait_ge(resid_added, 4 * (s.resid + i))
                            if s.pair:
                                dve.wait_ge(h_ready, s.pair)
                            sums(G, lambda m: ut[:, m])
                        elif g.kind == "gate":
                            if not (isinstance(i, int) and i + s.pair == 0):
                                dve.wait_ge(h_prod, s.pair + i)
                            sums(G, lambda m: gt[:, m])
                        elif g.kind == "up":
                            dve.wait_ge(h_ready, s.pair + i) if not (isinstance(i, int) and i + s.pair == 0) else None
                            dve.wait_ge(resid_added, 4 * s.resid)
                            sums(G, lambda m: ut[:, m])
                        elif g.kind == "glu_val":
                            if not (isinstance(i, int) and i == 0):
                                dve.wait_ge(glu_made, i)
                            sums(G, lambda m: ut[:, m])
                        elif g.kind == "glu_gate":
                            sums(G, lambda m: gt[:, m])
                        elif g.kind.startswith("fox"):
                            dst = (qT, kT, vT)[int(g.kind[3])]
                            sums(G, lambda m: dst[:, bass.ds(4 * i + m, 1), :].rearrange("p a t -> p (a t)"))
                        elif g.kind.startswith("gdn"):
                            short_conv_dve(dve, i, b, g, lambda dst: sums(G, dst))
                        if end and s.ahead:
                            split_lo(G + 1, 1, kc)
                        if g.kind == "gdn_z1":
                            gdn_dve(dve, i)
                rounds(dve, s, body, peel_first=s.early, peel_last=peel_last(s))
            norm_dve(dve, 4, split=False)

        def norm_dve(dve, n, split=True):
            dve.wait_ge(rms_ready, n + 1)
            nc.vector.reciprocal(rstd[:], rms[:]).then_inc(rstd_ready, 1)
            dve.wait_ge(rstd_ready, n + 1)
            g = NORM_COL[n]
            if n == 0:
                dve.wait_ge(const_cp, 4)

            def scale(c):
                for k in range(4):
                    kt = 4 * c + k
                    last = nc.vector.scalar_tensor_tensor(xn[:, c % 2, k] if split else xT[:, kt], xT[:, kt],
                                                          vec[:, g + kt:g + kt + 1], rstd[:], ALU.mult, ALU.mult)
                last.then_inc(xn_ready if split else y_made, 1)

            def lower(c):
                dve.wait_ge(xsh_ready, 4 * n + c + 1)
                nc.vector.tensor_tensor(xs[:, 4 * c:4 * c + 4, 1, :], xn[:, c % 2],
                                        xs[:, 4 * c:4 * c + 4, 0, :].bitcast(F32), ALU.subtract).then_inc(xs_ready, 1)
            if not split:
                for c in range(4):
                    scale(c)
                return
            scale(0)
            scale(1)
            lower(0)
            dve.wait_ge(xs_ready, 4 * n + 1)
            scale(2)
            lower(1)
            dve.wait_ge(xs_ready, 4 * n + 2)
            scale(3)
            lower(2)
            lower(3)

        def small_dve(dve, which, n):
            dve.wait_ge(wsm_hi, which + 1)
            nc.vector.tensor_tensor(wsm_s[:, :, n:2 * n], wsm[:, :, 0:n], wsm_s[:, :, 0:n].bitcast(F32), ALU.subtract)\
                .then_inc(wsm_lo, 1)
            dve.wait_ge(wsm_mm, which + 1)
            ps = aux[3][:, 0:4 * n].rearrange("p (t two n) -> p t two n", t=TT, two=2)
            nc.vector.tensor_copy(small[:, :, 0:n], ps[:, :, 1]).then_inc(sp_dve, 1)
            dve.wait_ge(sp_dve, SPD * which + 1)

        def softplus_dve(dve, base_, width):
            z, az, e, u, ln, d, m, r = (t[:, 0:width] for t in sp)
            steps = [base_]

            def link(ins):
                steps[0] += 1
                ins.then_inc(sp_dve, 1)
                dve.wait_ge(sp_dve, steps[0])
            return link

        def fox_gate_dve(dve):
            z, az, e, u, ln, d, m, r = (t[:] for t in sp)
            w = TT * HEADS0
            ps = aux[3][:, 0:4 * HEADS0].rearrange("p (t two n) -> p t two n", t=TT, two=2)
            s0 = small[:, :, 0:HEADS0]
            steps = [1]

            def link(ins):
                steps[0] += 1
                ins.then_inc(sp_dve, 1)
                dve.wait_ge(sp_dve, steps[0])

            def w2(t):
                return t[:, 0:w].rearrange("p (t h) -> p t h", t=TT)
            fb = bias[:, 0:HEADS0].unsqueeze(1).to_broadcast([P, TT, HEADS0])
            nc.vector.memset(az, 0.0)
            nc.vector.memset(u, 1.0)
            nc.vector.memset(z, 0.0)
            nc.vector.tensor_tensor(s0, ps[:, :, 0], s0, ALU.add).then_inc(fg_tmp, 1)
            dve.wait_ge(fg_tmp, 1)
            nc.vector.tensor_tensor(s0, s0, fb, ALU.add).then_inc(fg_tmp, 1)
            dve.wait_ge(fg_tmp, 2)
            link(nc.vector.tensor_scalar(w2(z), s0, -1.0, None, ALU.mult))
            softplus_steps(dve, link, z, az, e, u, ln, d, m, r, 0, s0, None)
            nc.vector.tensor_scalar(logf[:], w2(ln), -1.0, None, ALU.mult).then_inc(fox_lf, 1)

        def softplus_steps(dve, link, z, az, e, u, ln, d, m, r, which, s0, _):
            link(nc.vector.scalar_tensor_tensor(az, z, -1.0, z, ALU.mult, ALU.max))
            dve.wait_ge(sp_act, 2 * which + 1)
            link(nc.vector.tensor_scalar(u, e, 1.0, None, ALU.add))
            link(nc.vector.tensor_scalar(d, u, -1.0, None, ALU.add))
            link(nc.vector.tensor_scalar(m, d, 0.0, None, ALU.is_equal))
            link(nc.vector.tensor_tensor(d, d, m, ALU.add))
            link(nc.vector.reciprocal(r, d))
            dve.wait_ge(sp_act, 2 * which + 2)
            link(nc.vector.tensor_tensor(ln, ln, m, ALU.add))
            link(nc.vector.tensor_tensor(ln, ln, e, ALU.mult))
            link(nc.vector.tensor_tensor(ln, ln, r, ALU.mult))
            link(nc.vector.scalar_tensor_tensor(ln, z, 0.0, ln, ALU.max, ALU.add))

        def gates_dve(dve):
            z, az, e, u, ln, d, m, r = (t[:] for t in sp)
            ps = aux[3][:, 0:256].rearrange("p (t two n) -> p t two n", t=TT, two=2)
            nc.vector.tensor_tensor(small[:], ps[:, :, 0], small[:], ALU.add).then_inc(gg_dve, 1)
            dve.wait_ge(gg_dve, 1)
            steps = [SPD + 1]

            def link(ins):
                steps[0] += 1
                ins.then_inc(sp_dve, 1)
                dve.wait_ge(sp_dve, steps[0])

            def w2(t):
                return t.rearrange("p (t h) -> p t h", t=TT)

            def both(t):
                return t.unsqueeze(1).to_broadcast([P, TT, V_HEADS])
            link(nc.vector.tensor_tensor(w2(z), small[:, :, 32:64], both(bias[:, 40:72]), ALU.add))
            softplus_steps(dve, link, z, az, e, u, ln, d, m, r, 1, None, None)
            dve.wait_ge(gg_act, 2)
            nc.vector.scalar_tensor_tensor(gate_g[:], w2(ln), -1.0, both(small[:, 0, 0:32]), ALU.mult, ALU.mult)\
                .then_inc(gg_dve, 1)
            dve.wait_ge(gg_act, 4)
            nc.vector.tensor_tensor(gate_bg[:], gate_b[:], gate_ec[:], ALU.mult).then_inc(gg_dve, 1)
            dve.wait_ge(gg_pe, 2)
            nc.vector.tensor_tensor(gate_ed[:], aux[2][:, 0:64].rearrange("p (t h) -> p t h", t=TT), gate_c[:],
                                    ALU.subtract).then_inc(gg_dve, 1)

        def conv_taps(dve, i, n):
            for q in range(10 * n, 10 * n + 10):
                tap, ct = q // 8, q % 8
                k = 15 * i + tap + 1
                dve.wait_ge(conv_step, 120 * i + q + 1)
                nc.vector.scalar_tensor_tensor(conv[:, ct], u_pad[:, ct, bass.ds(k, T)],
                                               conv_w[:, bass.ds(k, 1), ct], conv[:, ct], ALU.mult, ALU.add)\
                    .then_inc(conv_step, 1)

        def ln_dve_steps(dve):
            dve.wait_ge(conv_step, 8 + 240)
            dve.wait_ge(ln_pe, 1)
            mean = aux[0][:, 0:T].unsqueeze(1).to_broadcast([P, CT, T])
            nc.vector.scalar_tensor_tensor(conv[:], mean, -1.0 / 1024, conv[:], ALU.mult, ALU.add).then_inc(ln_dve, 1)
            dve.wait_ge(ln_act, 2)
            nc.vector.reciprocal(rstd[:], rms[:]).then_inc(ln_dve, 1)
            dve.wait_ge(ln_dve, 2)
            nc.vector.tensor_tensor(conv[:], conv[:], rstd[:].unsqueeze(1).to_broadcast([P, CT, T]), ALU.mult)\
                .then_inc(ln_dve, 1)
            dve.wait_ge(ln_act, 4)
            nc.vector.tensor_tensor(hs[0][:, 8:16, 1, :], u_sq[:], hs[0][:, 8:16, 0, :].bitcast(F32), ALU.subtract)\
                .then_inc(ln_dve, 1)

        def fox_dve(dve):
            for h in range(HEADS0):
                p, n = h % 2, h // 2
                dve.wait_ge(fx_pe[p], 3 * n + 1)
                dve.wait_ge(fox_cp, 2)
                for t in range(TT):
                    last = nc.vector.tensor_scalar(sc[:, p, t, 0:P * (t + 1)], aux[2 * p][:, P * t:P * t + P * (t + 1)],
                                                   1.0 / math.sqrt(P), cq[:, t, h:h + 1], ALU.mult, ALU.add)
                last.then_inc(fx_dve[p], 1)
                dve.wait_ge(fx_pool[p], n + 1)
                for t in range(TT):
                    last = nc.vector.tensor_reduce(mx[:, p, t:t + 1], sc[:, p, t, 0:P * (t + 1)], AX.X, ALU.max,
                                                   negate=True)
                last.then_inc(fx_dve[p], 1)
                dve.wait_ge(fx_act[p], 4 * n + 2)
                nc.vector.reciprocal(rinv[:, p], rsum[:, p]).then_inc(fx_dve[p], 1)
                dve.wait_ge(fx_dve[p], 5 * n + 3)
                for t in range(TT):
                    w = sc[:, p, t, 0:P * (t + 1)]
                    last = nc.vector.tensor_scalar(w, w, rinv[:, p, t:t + 1], None, ALU.mult)
                last.then_inc(fx_dve[p], 1)
                dve.wait_ge(fx_act[p], 4 * n + 4)
                nc.vector.tensor_tensor(hs[0][:, h, 1, :], aux[2 * p][:, 0:T], hs[0][:, h, 0, :].bitcast(F32),
                                        ALU.subtract).then_inc(fx_dve[p], 1)

        def short_conv_dve(dve, j, b, g, sums):
            if not (isinstance(j, int) and j == 0 and b == 0):
                dve.wait_ge(conv_silu, 6 * j + b)
            n0 = 4 * (4 * j + b)
            if g.kind.startswith("gdn_z"):
                sums(lambda m: gt[:, m])
                return
            sums(lambda m: ut[:, m])
            ct = {"gdn_q": 4 * j, "gdn_k": 16 + 4 * j, "gdn_v0": 32 + 8 * j, "gdn_v1": 36 + 8 * j}[g.kind]
            dve.wait_ge(acc_free, 4 * (seg_of["in1"][0].first + 6 * j + b) + 4)
            for s in range(4):
                if s:
                    dve.wait_ge(sc_step, n0 + s)
                for m in range(GM):
                    w = short_w[:, 3 - s, bass.ds(ct + m, 1)]
                    if s == 0:
                        last = nc.vector.tensor_scalar(gt[:, m], ut[:, m], w, None, ALU.mult)
                    else:
                        last = nc.vector.scalar_tensor_tensor(gt[:, m, s:T], ut[:, m, 0:T - s], w, gt[:, m, s:T],
                                                              ALU.mult, ALU.add)
                last.then_inc(sc_step, 1)

        def gdn_dve(dve, j):
            dve.wait_ge(gg_act, 6)
            dve.wait_ge(l2_act, 5 * j + 5)
            nc.vector.reciprocal(qk_sq[:], qk_sq[:]).then_inc(l2_dve, 1)
            dve.wait_ge(l2_dve, 2 * j + 1)
            nc.vector.tensor_tensor(qk[:], qk[:], qk_sq[:], ALU.mult).then_inc(l2_dve, 1)
            for u in range(2):
                for step in gdn_dve_steps(dve, j, u):
                    pass

        def pairs(t, j, a):
            v = t[:, :, bass.ds(SV * j + 2 * a, 2)].rearrange("p t b -> p b t")
            return v.unsqueeze(3).to_broadcast([P, 2, TT, P])

        def four(t):
            return t.rearrange("p (b t) i -> p b t i", b=2)

        def bank(p, w):
            return aux[2 * p + w][:].rearrange("p (b t i) -> p b t i", b=2, t=TT)

        def over_b(t):
            return t.unsqueeze(1).to_broadcast([P, 2, TT, P])

        def gdn_dve_steps(dve, j, u):
            n = 2 * j + u
            ident4 = ident[:].unsqueeze(1).to_broadcast([P, 4, P])
            for p in range(2):
                dve.wait_ge(gd_pe[p], NP * n + P_GB)
                nc.vector.tensor_tensor(four(slot[p][0][:]), pairs(gate_c, j, 2 * u + p), bank(p, 0), ALU.subtract)\
                    .then_inc(gd_dve[p], 1)
            for p in range(2):
                dve.wait_ge(gd_pe[p], NP * n + P_KK)
                dve.wait_ge(gd_act[p], NA * n + A_DECAY)
                kk = aux[2 * p + 1][:, 0:256].rearrange("p (t i) -> p t i", t=TT)
                qq = aux[2 * p + 1][:, 256:512].rearrange("p (t i) -> p t i", t=TT)
                nc.vector.tensor_tensor(four(slot[p][1][:]), over_b(kk), four(slot[p][0][:]), ALU.mult)\
                    .then_inc(gd_dve[p], 1)
                nc.vector.tensor_tensor(four(slot[p][2][:]), over_b(qq), four(slot[p][0][:]), ALU.mult)\
                    .then_inc(gd_dve[p], 1)
            for p in range(2):
                dve.wait_ge(gd_pool[p], NO * n + O_R1)
                nc.vector.tensor_tensor(slot[p][5][:], ident4, slot[p][5][:], ALU.subtract).then_inc(gd_dve[p], 1)
                dve.wait_ge(gd_pool[p], NO * n + O_Q1)
                nc.vector.tensor_tensor(slot[p][6][:], ident4, slot[p][6][:], ALU.subtract).then_inc(gd_dve[p], 1)
            for lv in range(1, LEVELS):
                for p in range(2):
                    dve.wait_ge(gd_pe[p], NP * n + P_LV(lv, 1))
                    w = slot[p][5] if lv < LEVELS - 1 else slot[p][6]
                    nc.vector.tensor_tensor(flat(w[:]), flat(w[:]), aux[2 * p + 1][:], ALU.subtract)\
                        .then_inc(gd_dve[p], 1)
            for p in range(2):
                a = 2 * u + p
                dve.wait_ge(gd_pe[p], NP * n + P_KT)
                kt = aux[2 * p][:, 0:256].rearrange("p (t i) -> p t i", t=TT)
                nc.vector.tensor_tensor(four(slot[p][1][:]), over_b(kt), pairs(gate_bg, j, a), ALU.mult)\
                    .then_inc(gd_dve[p], 1)
                nc.vector.tensor_tensor(four(slot[p][2][:]), over_b(kt), pairs(gate_ed, j, a), ALU.mult)\
                    .then_inc(gd_dve[p], 1)
                nc.vector.tensor_tensor(four(slot[p][0][:]), bank(p, 1), pairs(gate_b, j, a), ALU.mult)\
                    .then_inc(gd_dve[p], 1)
            for c in range(4):
                t, r = c // 2, slice(64 * (c % 2), 64 * (c % 2) + 64)
                for p in range(2):
                    if c:
                        dve.wait_ge(gd_pe[p], NP * n + P_WS(c))
                        dve.wait_ge(gd_act[p], NA * n + A_U)
                        v = four(slot[p][4][:])[r, :, t, :]
                        nc.vector.tensor_tensor(v, v, aux[2 * p][r, 0:256].rearrange("p (b i) -> p b i", b=2),
                                                ALU.subtract).then_inc(gd_dve[p], 1)
                if c < 3:
                    for p in range(2):
                        a = 2 * u + p
                        dve.wait_ge(gd_pe[p], NP * n + P_DS(c))
                        for b in range(2):
                            ds_ = aux[2 * p + 1][:, b * P:(b + 1) * P]
                            if c == 0:
                                i_ = nc.vector.tensor_copy(state[p][:, b], ds_)
                            else:
                                i_ = nc.vector.scalar_tensor_tensor(
                                    state[p][:, b], state[p][:, b], gate_el[:, c, bass.ds(SV * j + 2 * a + b, 1)],
                                    ds_, ALU.mult, ALU.add)
                        i_.then_inc(gd_dve[p], 1)
            for p in range(2):
                dve.wait_ge(gd_pe[p], NP * n + P_O)
                dve.wait_ge(gd_act[p], NA * n + A_QS)
                dve.wait_ge(gd_pool[p], NO * n + O_ZERO)
                nc.vector.tensor_tensor(flat(slot[p][0][:]), aux[2 * p][:], flat(slot[p][1][:]), ALU.add)\
                    .then_inc(gd_dve[p], 1)
            for p in range(2):
                dve.wait_ge(gd_pool[p], NO * n + O_SQ)
                nc.vector.tensor_reduce(o_ss[:, p], slot[p][1][:], AX.X, ALU.add).then_inc(gd_dve[p], 1)
            for p in range(2):
                dve.wait_ge(gd_act[p], NA * n + A_RMS)
                nc.vector.reciprocal(o_rs[:, p], o_rs[:, p]).then_inc(gd_dve[p], 1)
            for p in range(2):
                a = 2 * u + p
                dve.wait_ge(gd_pe[p], NP * n + P_OT)
                nc.vector.scalar_tensor_tensor(
                    og[:, bass.ds(SV * j + 2 * a, 2), :].rearrange("p b t -> p (b t)"), aux[2 * p + 1][:],
                    vec[:, ON:ON + 1], zs[:, 2 * a:2 * a + 2, :].rearrange("p b t -> p (b t)"), ALU.mult, ALU.mult)\
                    .then_inc(gd_dve[p], 1)
            yield

        def gdn_pool(pool, j):
            pool.wait_ge(gg_dve, 4)
            pool.wait_ge(gg_act, 6)
            if not (isinstance(j, int) and j == 0):
                for p in range(2):
                    pool.wait_ge(gd_pe[p], NP * 2 * j)
            apart(pool)
            nc.gpsimd.tensor_copy(g_set[:], gate_g[:, :, bass.ds(SV * j, SV)]).then_inc(gset_ready, 1)
            for u in range(2):
                for step in gdn_pool_steps(pool, j, u):
                    pass

        def gdn_pool_steps(pool, j, u):
            n = 2 * j + u

            def mask4(m):
                return m.unsqueeze(1).to_broadcast([P, 4, P])
            for p in range(2):
                pool.wait_ge(gd_dve[p], ND * n + D_DIFF)
                s0 = slot[p][0]
                nc.gpsimd.tensor_tensor(s0[:], s0[:], mask4(mask_gdn[:]), ALU.add).then_inc(gd_pool[p], 1)
            for p in range(2):
                a = 2 * u + p
                pool.wait_ge(gd_dve[p], ND * n + D_KK)
                apart(pool)
                s1 = four(slot[p][1][:])
                nc.gpsimd.tensor_tensor(s1, s1, pairs(gate_b, j, a), ALU.mult).then_inc(gd_pool[p], 1)
            for p in range(2):
                pool.wait_ge(gd_pool[p], NO * n + O_BETA)
                nc.gpsimd.tensor_tensor(slot[p][5][:], slot[p][1][:], mask4(lvl0t[:]), ALU.mult)\
                    .then_inc(gd_pool[p], 1)
                pool.wait_ge(gd_act[p], NA * n + A_LT)
                nc.gpsimd.tensor_tensor(slot[p][6][:], slot[p][4][:], mask4(lvl[:, 0, :]), ALU.mult)\
                    .then_inc(gd_pool[p], 1)
            for lv in range(1, LEVELS):
                for p in range(2):
                    if lv == 1:
                        pool.wait_ge(gd_dve[p], ND * n + D_QK)
                    elif lv == 2:
                        pool.wait_ge(gd_pe[p], NP * n + P_LT)
                        pool.wait_ge(gd_pool[p], NO * n + O_R1)
                    else:
                        pool.wait_ge(gd_pe[p], NP * n + P_LV(lv - 2, 0))
                    nc.gpsimd.tensor_tensor(slot[p][(lv + 1) % 2][:], slot[p][4][:], mask4(lvl[:, lv, :]), ALU.mult)\
                        .then_inc(gd_pool[p], 1)
            for p in range(2):
                pool.wait_ge(gd_pe[p], NP * n + P_W)
                apart(pool)
                pool.memset(four(slot[p][1][:])[0:64, :, 0, :], 0.0).then_inc(gd_pool[p], 1)
            for p in range(2):
                pool.wait_ge(gd_dve[p], ND * n + D_O)
                nc.gpsimd.tensor_tensor(slot[p][1][:], slot[p][0][:], slot[p][0][:], ALU.mult)\
                    .then_inc(gd_pool[p], 1)
            for p in range(2):
                pool.wait_ge(gd_dve[p], ND * n + D_RS)
                rs = o_rs[:, p].unsqueeze(2).to_broadcast([P, 4, P])
                nc.gpsimd.tensor_tensor(slot[p][0][:], slot[p][0][:], rs, ALU.mult).then_inc(gd_pool[p], 1)
            yield

        def fox_pool(pool):
            for h in range(HEADS0):
                p, n = h % 2, h // 2
                pool.wait_ge(fx_dve[p], 5 * n + 1)
                diag = sc[:, p, :, :].rearrange("p t k -> p (t k)")
                for t in range(TT):
                    w = sc[:, p, t, P * t:P * (t + 1)]
                    last = nc.gpsimd.tensor_tensor(w, w, mask_fox[:], ALU.add)
                last.then_inc(fx_pool[p], 1)

        def tensor_program(pe):
            mm, tr = nc.tensor.matmul, nc.tensor.transpose

            pe.wait_ge(const_in, 16 * 15)
            pe.wait_ge(const_step, N_CONST_PE)
            tr(aux[0][:, 0:NVEC], vrow[0:NVEC, 0, :], ident[0:NVEC, 0:NVEC]).then_inc(const_pe, 1)
            tr(aux[1][:, 0:124], vrow[0:124, 1, :], ident[0:124, 0:124]).then_inc(const_pe, 1)
            tr(aux[1][:, 124:248], vrow[0:124, 2, :], ident[0:124, 0:124]).then_inc(const_pe, 1)
            tr(aux[2][:, 0:128], vrow[:, 3, :], ident[:]).then_inc(const_pe, 1)
            tr(aux[2][:, 128:256], vrow[:, 4, :], ident[:]).then_inc(const_pe, 1)
            mm(aux[3][:, 0:72], ones[0:1, :], brow[:], start=True, stop=True).then_inc(const_pe, 1)
            pe.wait_ge(const_step, N_CONST)
            pe.wait_ge(x_in, 16)
            for k in range(0, KT, 2):
                if k >= 8:
                    pe.wait_ge(x_copied, k - 6)
                for h in range(2):
                    for t in range(TT):
                        last = tr(acc[:, (k // 2) % 4, h * T + t * P:h * T + (t + 1) * P],
                                  stage[:, t, (k + h) * P:(k + h + 1) * P], ident[:])
                last.then_inc(x_trans, 1)

            def norm(n):
                pe.wait_ge(sq_added, 16 * n + 16)
                if n == 0:
                    pe.wait_ge(const_cp, 1)
                mm(aux[0][:, 0:T], ones[:], sq_acc[:], start=True, stop=True).then_inc(ss_ready, 1)

            def narrow(which, n, ns):
                pe.wait_ge(wsm_lo, which + 1)
                pe.wait_ge(xs_ready, 4 * ns + 4)
                if which == 0:
                    pe.wait_ge(const_cp, 4)
                for t in range(TT):
                    o = aux[3][:, 2 * n * t:2 * n * (t + 1)]
                    for k in range(KT):
                        fr = slice(t * P, (t + 1) * P)
                        mm(o, xs[:, k, 0, fr], wsm_s[:, k, 0:2 * n], start=k == 0, stop=k == KT - 1,
                           skip_group_check=True)
                        last = mm(o[:, 0:n], xs[:, k, 1, fr], wsm_s[:, k, 0:n], start=False, stop=k == KT - 1,
                                  skip_group_check=True)
                last.then_inc(wsm_mm, 1)

            def group(s, i, b, g):
                G = number(s, i, b)
                r = rhs_of(g)
                for c in range(NCH):
                    pe.wait_ge(lo_ready, 4 * G + c + 1)
                    if s.early and b == 0:
                        pe.wait_ge(xs_ready, 4 * g.norm + c + 1)
                    if s.name in ("out1a", "out1b"):
                        pe.wait_ge(og_ready, 4 * int(s.name == "out1b") + c + 1)
                    if s.name.startswith("down"):
                        pe.wait_ge(h_ready, DOWN_NEEDS(s, g))
                    if s.name == "out0" and c == 0:
                        pe.wait_ge(ln_dve, 4)
                        for p in range(2):
                            pe.wait_ge(fx_dve[p], 5 * HEADS0 // 2)
                    for m in range(GM):
                        if c == 0:
                            if isinstance(G, int) and G == 0:
                                pe.wait_ge(x_copied, KT)
                            else:
                                pe.wait_ge(acc_free, 4 * G + m - 3)
                        for k in range(g.kc):
                            kk = g.kc * c + k
                            end = kk == NCH * g.kc - 1
                            cols = slice(m * P, (m + 1) * P)
                            mm(acc[:, m, :], w_hi[:, c % 2, k, cols], r[:, kk], start=kk == 0, stop=end,
                               skip_group_check=True)
                            last = mm(acc[:, m, T:2 * T], w_lo[:, c % 2, k, cols], r[:, kk, 0], start=False,
                                      stop=end, skip_group_check=True)
                        if c == NCH - 1:
                            last.then_inc(acc_ready, 1)
                    if c < NCH - 1:
                        last.then_inc(w_used, 1)

            for s in segs:
                g0 = s.groups[0]
                if s.early:
                    norm(g0.norm)
                if s.name == "glu":
                    narrow(0, HEADS0, 0)
                    pe.wait_ge(fox_lf, 1)
                    for t in range(TT):
                        o = aux[2][:, 8 * t:8 * t + 8]
                        o2 = aux[1][0:HEADS0, t * P:(t + 1) * P]
                        for q in range(t + 1):
                            w = triu if q == t else ones
                            mm(o, w[:], logf[:, q], start=q == 0, stop=q == t)
                    for t in range(TT):
                        o2 = aux[1][0:HEADS0, t * P:(t + 1) * P]
                        for q in range(t + 1):
                            w = triu if q == t else ones
                            last = mm(o2, logf[:, q], w[:], start=q == 0, stop=q == t)
                    last.then_inc(fox_pe0, 1)
                if s.name == "out0":
                    pe.wait_ge(conv_step, 8 + 240)
                    for c in range(CT):
                        last = mm(aux[0][:, 0:T], ones[:], conv[:, c], start=c == 0, stop=c == CT - 1)
                    last.then_inc(ln_pe, 1)
                    pe.wait_ge(ln_act, 1)
                    for c in range(CT):
                        last = mm(aux[1][:, 0:T], ones[:], u_sq[:, c], start=c == 0, stop=c == CT - 1)
                    last.then_inc(ln_pe, 1)
                    fox_pe_steps(pe, mm, tr, s)
                if s.name == "in1":
                    narrow(1, 64, 2)
                    pe.wait_ge(gg_dve, 2)
                    for t in range(TT):
                        mm(aux[1][:, 32 * t:32 * t + 32], chunk_triu[:], gate_g[:, t], start=True, stop=True)
                    for t in range(TT):
                        last = mm(aux[2][:, 32 * t:32 * t + 32], chunk_ones[:], gate_g[:, t], start=True, stop=True)
                    last.then_inc(gg_pe, 1)
                    for c in range(4):
                        mine = chunk_ones[:, 64 * (c % 2):64 * (c % 2) + 1].to_broadcast([P, P])
                        last = mm(aux[3][:, 32 * c:32 * c + 32], mine, gate_g[:, c // 2], start=True, stop=True)
                    last.then_inc(gg_pe, 1)

                def body(i, last_, s=s):
                    for b, g in enumerate(s.groups):
                        group(s, i, b, g)
                        if g.kind == "gdn_z1":
                            gdn_pe(pe, mm, tr, i)
                rounds(pe, s, body, peel_first=s.first == 0)
            norm(4)
            for k in range(KT // 2):
                pe.wait_ge(y_made, k // 2 + 1)
                if k >= 2:
                    pe.wait_ge(y_out, 2 * k - 2)
                for t in range(TT):
                    for h in range(2):
                        last = tr(aux[(2 * k + t) % 4][:, h * P:(h + 1) * P], xT[:, 2 * k + h, t * P:(t + 1) * P], ident[:])
                last.then_inc(y_pe, 1)

        def DOWN_NEEDS(s, g):
            layer_pairs = 0 if s.resid < 16 else 11
            return layer_pairs + min(11, 4 * (g.at + 1))

        def fox_pe_steps(pe, mm, tr, s):
            pe.wait_ge(acc_free, 4 * s.first)
            for h in range(HEADS0):
                if h >= 2:
                    pe.wait_ge(vt_act, h - 1)
                elif h == 0:
                    pe.wait_ge(ln_dve, 1)
                else:
                    pe.wait_ge(ln_act, 2)
                for t in range(TT):
                    last = tr(aux[h % 2][:, t * P:(t + 1) * P], vT[:, h, t * P:(t + 1) * P], ident[:])
                last.then_inc(vt_pe, 1)
            for h in range(HEADS0):
                p, n = h % 2, h // 2
                A, B = aux[2 * p], aux[2 * p + 1]
                if h >= 2:
                    pe.wait_ge(fx_dve[p], 5 * n)
                else:
                    pe.wait_ge(vt_act, HEADS0)
                pe.wait_ge(fox_cp, 2)
                sel = ident[0:HEADS0, h:h + 1].to_broadcast([HEADS0, P])
                for t in range(TT):
                    o = A[:, P * t:P * t + P * (t + 1)]
                    mm(o, qT[:, h, t * P:(t + 1) * P], kT[:, h, 0:P * (t + 1)], start=True, stop=False)
                    last = mm(o, sel, ncT[:, 0:P * (t + 1)], start=False, stop=True)
                last.then_inc(fx_pe[p], 1)
                pe.wait_ge(fx_dve[p], 5 * n + 4)
                tr(B[:, 0:P], sc[:, p, 0, 0:P], ident[:])
                for q in range(TT):
                    last = tr(B[:, P * (q + 1):P * (q + 2)], sc[:, p, 1, q * P:(q + 1) * P], ident[:])
                last.then_inc(fx_pe[p], 1)
                pe.wait_ge(fx_act[p], 4 * n + 3)
                mm(A[:, 0:T], v_tok[:, h, 0], pT[:, p, 0:T], start=True, stop=False, skip_group_check=True)
                mm(A[:, P:T], v_tok[:, h, 1], pT[:, p, T:T + P], start=False, stop=True, skip_group_check=True)\
                    .then_inc(fx_pe[p], 1)

        def gdn_pe(pe, mm, tr, j):
            pe.wait_ge(l2_act, 5 * j + 1)
            for n in range(4):
                last = mm(aux[n][:], ones[:], qk_sq[:, n // 2, 2 * (n % 2):2 * (n % 2) + 2, :], start=True, stop=True)
            last.then_inc(l2_pe, 1)
            pe.wait_ge(gset_ready, j + 1)
            pe.wait_ge(l2_dve, 2 * j + 2)
            for u in range(2):
                for step in gdn_pe_steps(pe, mm, tr, j, u):
                    pass

        def gdn_pe_steps(pe, mm, tr, j, u):
            n = 2 * j + u

            def fr(t):
                return slice(t * P, (t + 1) * P)
            for p in range(2):
                a = 2 * u + p
                A, B = aux[2 * p], aux[2 * p + 1]
                if u:
                    pe.wait_ge(gd_dve[p], ND * n)
                for b in range(2):
                    for t in range(TT):
                        g = g_set[:, t, 2 * a + b:2 * a + b + 1].to_broadcast([P, P])
                        last = mm(A[:, fr(2 * b + t)], g, chunk_triu[:], start=True, stop=True)
                last.then_inc(gd_pe[p], 1)
                for t in range(TT):
                    mm(B[:, fr(t)], qk[:, 1, a, fr(t)], qk[:, 1, a, fr(t)], start=True, stop=True)
                for t in range(TT):
                    last = mm(B[:, fr(2 + t)], qk[:, 0, a, fr(t)], qk[:, 1, a, fr(t)], start=True, stop=True)
                last.then_inc(gd_pe[p], 1)
            for p in range(2):
                A, B = aux[2 * p], aux[2 * p + 1]
                pe.wait_ge(gd_pool[p], NO * n + O_BETA)
                for q in range(4):
                    last = tr(A[:, fr(q)], slot[p][1][:, q], ident[:])
                last.then_inc(gd_pe[p], 1)
                pe.wait_ge(gd_dve[p], ND * n + D_QK)
                for q in range(4):
                    last = tr(B[:, fr(q)], slot[p][2][:, q], ident[:])
                last.then_inc(gd_pe[p], 1)
            for lv in range(1, LEVELS):
                for p in range(2):
                    pe.wait_ge(gd_pool[p], NO * n + O_M(lv))
                    pe.wait_ge(gd_dve[p], ND * n + (D_Q1 if lv == 1 else D_LV(lv - 1)))
                    if lv > 1:
                        pe.wait_ge(gd_act[p], NA * n + A_LV(lv - 1, 1))
                    else:
                        pe.wait_ge(gd_act[p], NA * n + A_IT)
                    for q in range(4):
                        last = mm(aux[2 * p][:, fr(q)], slot[p][(lv + 1) % 2][:, q], slot[p][5][:, q], start=True, stop=True)
                    last.then_inc(gd_pe[p], 1)
                for p in range(2):
                    pe.wait_ge(gd_act[p], NA * n + A_LV(lv, 0))
                    for q in range(4):
                        w, r = (slot[p][6], slot[p][2]) if lv < LEVELS - 1 else (slot[p][2], slot[p][6])
                        last = mm(aux[2 * p + 1][:, fr(q)], w[:, q], r[:, q], start=True, stop=True)
                    last.then_inc(gd_pe[p], 1)
                if lv < LEVELS - 1:
                    for p in range(2):
                        pe.wait_ge(gd_dve[p], ND * n + D_LV(lv))
                        for q in range(4):
                            last = tr(aux[2 * p][:, fr(q)], slot[p][5][:, q], ident[:])
                        last.then_inc(gd_pe[p], 1)
            for p in range(2):
                a = 2 * u + p
                A, B = aux[2 * p], aux[2 * p + 1]
                for t in range(TT):
                    last = tr(A[:, fr(t)], qk[:, 1, a, fr(t)], ident[:])
                pe.wait_ge(gd_dve[p], ND * n + D_LV(LEVELS - 1))
                for b in range(2):
                    for t in range(TT):
                        last = tr(B[:, fr(2 * b + t)], vs[:, 2 * a + b, fr(t)], ident[:])
                last.then_inc(gd_pe[p], 1)
            for p in range(2):
                A, B = aux[2 * p], aux[2 * p + 1]
                pe.wait_ge(gd_dve[p], ND * n + D_VB)
                for q in range(4):
                    last = mm(A[:, fr(q)], slot[p][6][:, q], slot[p][0][:, q], start=True, stop=True)
                last.then_inc(gd_pe[p], 1)
                for q in range(4):
                    last = mm(B[:, fr(q)], slot[p][1][:, q], slot[p][6][:, q], start=True, stop=True)
                last.then_inc(gd_pe[p], 1)
            for c in range(4):
                t, r = c // 2, slice(64 * (c % 2), 64 * (c % 2) + 64)
                if c:
                    for p in range(2):
                        a = 2 * u + p
                        A = aux[2 * p]
                        pe.wait_ge(gd_dve[p], ND * n + D_S(c - 1))
                        pe.wait_ge(gd_act[p], NA * n + (A_W if c == 1 else A_QC(c - 1)))
                        for b in range(2):
                            mm(A[:, fr(b)], slot[p][5][:, 2 * b + t], state[p][:, b], start=True, stop=True)
                        mm(A[:, T:2 * T], qk[:, 0, a, fr(t)], state[p][:], start=True, stop=True)\
                            .then_inc(gd_pe[p], 1)
                if c < 3:
                    for p in range(2):
                        B = aux[2 * p + 1]
                        if c:
                            pe.wait_ge(gd_dve[p], ND * n + D_VN(c))
                        else:
                            pe.wait_ge(gd_act[p], NA * n + A_W)
                        for b in range(2):
                            last = mm(B[:, fr(b)], slot[p][2][r, 2 * b + t], slot[p][4][r, 2 * b + t], start=True, stop=True)
                        last.then_inc(gd_pe[p], 1)
            for p in range(2):
                pe.wait_ge(gd_dve[p], ND * n + D_VN(3))
                pe.wait_ge(gd_act[p], NA * n + A_QS)
                for q in range(4):
                    last = mm(aux[2 * p][:, fr(q)], slot[p][3][:, q], slot[p][4][:, q], start=True, stop=True)
                last.then_inc(gd_pe[p], 1)
            for p in range(2):
                pe.wait_ge(gd_pool[p], NO * n + O_ON)
                for q in range(4):
                    last = tr(aux[2 * p + 1][:, fr(q)], slot[p][0][:, q], ident[:])
                last.then_inc(gd_pe[p], 1)
            yield


        block = ctx.enter_context(nc.Block())

        @block.sync
        def _(eng):
            sync_program(eng)

        @block.gpsimd
        def _(eng):
            pool_program(eng)

        @block.scalar
        def _(eng):
            scalar_program(eng)

        @block.vector
        def _(eng):
            vector_program(eng)

        @block.tensor
        def _(eng):
            tensor_program(eng)


SPD = 12
N_CONST = 40
N_CONST_PE = 3

P_GB, P_KK, P_LT, P_IT = 1, 2, 3, 4


def P_LV(lv, k):
    return 4 + 3 * (lv - 1) + k + 1


P_KT = P_LV(LEVELS - 1, 1) + 1
P_U, P_W = P_KT + 1, P_KT + 2


def P_DS(c):
    return P_W + 1 + 2 * c


def P_WS(c):
    return P_W + 2 * c


P_O = P_WS(3) + 1
P_OT = P_O + 1
NP = P_OT

A_DECAY, A_LT, A_IT = 1, 2, 3


def A_LV(lv, k):
    return 3 + 2 * (lv - 1) + k + 1


A_U = A_LV(LEVELS - 1, 0) + 1
A_W = A_U + 1


def A_QC(c):
    return A_W + 2 * c


A_QS = A_QC(3)
A_RMS = A_QS + 1
NA = A_RMS

D_DIFF, D_KK, D_QK, D_R1, D_Q1 = 1, 2, 3, 4, 5


def D_LV(lv):
    return 5 + lv


D_KBG, D_KDEC, D_VB = (D_LV(LEVELS - 1) + n for n in (1, 2, 3))


def D_S(c):
    return D_VB + 1 + 2 * c


def D_VN(c):
    return D_VB + 2 * c


D_O = D_VN(3) + 1
D_SS, D_RS, D_OG = D_O + 1, D_O + 2, D_O + 3
ND = D_OG

O_MASK, O_BETA, O_R1, O_Q1 = 1, 2, 3, 4


def O_M(lv):
    return 4 + lv


O_ZERO = O_M(LEVELS - 1) + 1
O_SQ, O_ON = O_ZERO + 1, O_ZERO + 2
NO = O_ON

_INS = ["x", "norm_mix0", "w_in0", "fgate_bias0", "conv_w0", "conv_b0", "conv_ln_g0", "conv_ln_b0", "w_out0",
        "norm_mix1", "w_in1", "short_conv1", "a_log1", "dt_bias1", "o_norm1", "w_out1",
        "norm_ffn", "w_gate", "w_up", "w_down", "final_norm"]


def kernel(**inputs):
    import numpy as _np
    import concourse.bacc as _bacc
    from concourse import mybir as _mybir
    from concourse.bass_utils import run_bass_kernel_spmd as _run

    nc = _bacc.Bacc("TRN2", target_bir_lowering=False, num_devices=1)
    arrays, args = {}, []
    for name in _INS:
        a = _np.ascontiguousarray(inputs[name])
        arrays[f"in_{name}"] = a
        args.append(nc.dram_tensor(f"in_{name}", a.shape, _mybir.dt.from_np(a.dtype), kind="ExternalInput").ap())
    save = nc.dram_tensor("x_save", (D, T), _mybir.dt.float32, kind="Internal").ap()
    out = nc.dram_tensor("out", (1, T, D), _mybir.dt.float32, kind="ExternalOutput").ap()
    trunk(nc, *args, save, out)
    r = _run(nc, [arrays], core_ids=[0])
    return r.results[0]["out"]
```

```python
import math
from contextlib import ExitStack

import concourse.bass as bass
from concourse import mybir

F32 = mybir.dt.float32
F32R = mybir.dt.float32r
BF16 = mybir.dt.bfloat16
ALU = mybir.AluOpType
ACT = mybir.ActivationFunctionType
AX = mybir.AxisListType

P = 128
T = 256
TT = T // P
D = 2048
KT = D // P
GW = 512
GM = GW // P
NCH = 4
EPS = 1e-6
NEG = -1e30

HEADS0 = 8
CONV_W = 31
CT = 8
F_COL = 3 * 1024
GLU_COL = F_COL + HEADS0
QK_HEADS = 16
V_HEADS = 32
SETS = 4
SQ = QK_HEADS // SETS
SV = V_HEADS // SETS
BA_COL = 12288
DFF = 5632
LEVELS = 6

G_MIX0, G_MIX1, G_FFN0, G_FFN1, G_FINAL = 0, 16, 32, 48, 64
CB, LG, LB, ON, NVEC = 80, 88, 96, 104, 105
NORM_COL = (G_MIX0, G_FFN0, G_MIX1, G_FFN1, G_FINAL)


class Group:

    def __init__(self, w, col, rhs, kind, kc=4, row=0, step=0, at=0, norm=None):
        self.w, self.col, self.rhs, self.kind = w, col, rhs, kind
        self.kc, self.row, self.step, self.at, self.norm = kc, row, step, at, norm


class Segment:

    def __init__(self, name, n, groups, deltanet=False):
        self.name, self.n, self.groups = name, n, groups
        self.deltanet = deltanet
        self.scaled_of = [b for b, g in enumerate(groups) if g.kind != "resid"]
        self.conv_of = [b for b, g in enumerate(groups) if g.kind[:5] in ("gdn_q", "gdn_k", "gdn_v")]
        self.silu_of = [b for b, g in enumerate(groups) if g.kind.startswith("gdn")]


class Place:

    def __init__(self, s, i, b):
        self.s, self.i, self.b, self.g = s, i, b, s.groups[b]
        self.G = s.first + len(s.groups) * i + b

    def count(self, base, which):
        return base + len(which) * self.i + which.index(self.b)

    @property
    def scaled(self):
        return self.count(self.s.scaled, self.s.scaled_of)

    @property
    def conv(self):
        return self.count(self.s.conv, self.s.conv_of)

    @property
    def silu(self):
        return self.count(self.s.silu, self.s.silu_of)

    @property
    def starts(self):
        return isinstance(self.i, int) and self.i == 0 and self.b == 0


def plan():
    def ffn(layer, norm):
        def gu(p, n):
            c = p * 2048
            return Segment(f"gu{p}", n, [
                Group(f"gate{layer}", c, "x", "gate", step=GW, norm=norm),
                Group(f"up{layer}", c, "x", "up", step=GW, at=p)])

        def down(p, final=None):
            kc = 4 if p < 2 else 3
            return Segment(f"down{p}", 4, [
                Group(f"down{layer}", 0, f"h{p % 2}", "resid", kc=kc, row=p * 2048, step=GW, norm=final, at=p)])
        return [gu(0, 4), gu(1, 4), down(0), gu(2, 3), down(1), down(2, norm + 1)]

    def z(j):
        return [Group("in1", 8192 + 1024 * j, "x", "gdn_z0", step=1024),
                Group("in1", 8192 + 1024 * j + GW, "x", "gdn_z1", step=1024)]

    def qkv(j):
        return [Group("in1", GW * j, "x", "gdn_q", step=GW, norm=2),
                Group("in1", 2048 + GW * j, "x", "gdn_k", step=GW),
                Group("in1", 4096 + 1024 * j, "x", "gdn_v0", step=1024),
                Group("in1", 4096 + 1024 * j + GW, "x", "gdn_v1", step=1024)]

    segs = [Segment("glu", 2, [Group("in0", GLU_COL, "x", "glu_val", step=GW, norm=0),
                               Group("in0", GLU_COL + 1024, "x", "glu_gate", step=GW)]),
            Segment("qkv", 2, [Group("in0", 1024 * n, "x", f"fox{n}", step=GW) for n in range(3)]),
            Segment("out0", 4, [Group("out0", 0, "h0", "resid", step=GW, norm=1)])]
    segs += ffn(0, 1)
    segs += [Segment("in1_first", 1, qkv(0)),
             Segment("in1", SETS - 1, z(0) + qkv(1), deltanet=True),
             Segment("in1_last", 1, z(SETS - 1) + [Group("out1", GW * n, "x", "resid", at=n) for n in range(4)],
                     deltanet=True),
             Segment("out1b", 4, [Group("out1", 0, "h0", "resid", row=2048, step=GW, norm=3)])]
    segs += ffn(1, 3)
    at = resid = pair = scaled = conv = silu = 0
    for n, s in enumerate(segs):
        s.first, s.scaled, s.conv, s.silu = at, scaled, conv, silu
        at += s.n * len(s.groups)
        scaled += s.n * len(s.scaled_of)
        conv += s.n * len(s.conv_of)
        silu += s.n * len(s.silu_of)
        s.next_kc = segs[n + 1].groups[0].kc if n + 1 < len(segs) else 0
        s.resid, s.pair = resid, pair
        resid += s.n * sum(g.kind == "resid" for g in s.groups)
        if s.groups[0].kind == "gate":
            pair += s.n
    return segs


def trunk(nc, x, norm_mix0, w_in0, fgate_bias0, conv_w0, conv_b0, conv_ln_g0, conv_ln_b0, w_out0,
          norm_mix1, w_in1, short_conv1, a_log1, dt_bias1, o_norm1, w_out1,
          norm_ffn, w_gate, w_up, w_down, final_norm, og_save, out):
    weights = {"in0": w_in0[0], "out0": w_out0[0], "in1": w_in1[0], "out1": w_out1[0]}
    for layer in range(2):
        weights[f"gate{layer}"] = w_gate[layer]
        weights[f"up{layer}"] = w_up[layer]
        weights[f"down{layer}"] = w_down[layer]
    segs = plan()
    seg_of = {}
    for n, s in enumerate(segs):
        seg_of.setdefault(s.name, []).append(s)
    n_groups = sum(s.n * len(s.groups) for s in segs)

    ctx = ExitStack()
    with ctx:
        top = [0]

        def region(size):
            at = top[0]
            top[0] += size
            return at

        def sb(name, shape, dt=F32, at=None):
            size = 2 if dt == BF16 else 4
            for s in shape[1:]:
                size *= s
            if at is None:
                at = region((size + 31) // 32 * 32)
            return nc.alloc_sbuf_tensor_at(name, shape, dt, offset=base + at)

        base = (nc.sbuf_base + 31) // 32 * 32
        raw = sb("raw", [P, NCH, 4, GW])
        w_hi = sb("w_hi", [P, 2, 4, GW], F32R)
        w_lo = sb("w_lo", [P, 2, 4, GW], F32R)
        x_at = region(KT * 2 * T * 4)
        xs = sb("xs", [P, KT, 2, T], F32R, at=x_at)
        h_at = region(2 * KT * 2 * T * 4)
        hs = [sb(f"hs{p}", [P, KT, 2, T], F32R, at=h_at + p * 32768) for p in range(2)]
        r_at = region(KT * T * 4)
        xT = sb("xT", [P, KT, T], at=r_at)
        xn_at = region(8192)
        xn = sb("xn", [P, 2, 4, T], at=xn_at)
        ut = sb("ut", [P, GM, T])
        gt = sb("gt", [P, GM, T])
        tmp = sb("tmp", [P, 2, T])
        sq_acc = sb("sq_acc", [P, T])
        sq_one = sb("sq_one", [P, T])
        rms = sb("rms", [P, T])
        rstd = sb("rstd", [P, T])
        ident = sb("ident", [P, P])
        ones = sb("ones", [P, P])
        triu = sb("triu", [P, P])
        chunk_triu = sb("chunk_triu", [P, P])
        chunk_ones = sb("chunk_ones", [P, P])
        mask_fox = sb("mask_fox", [P, P])
        mask_gdn = sb("mask_gdn", [P, P])
        lvl = sb("lvl", [P, LEVELS, P], BF16)
        lvl0t = sb("lvl0t", [P, P], BF16)
        vec = sb("vec", [P, NVEC])
        conv_w = sb("conv_w", [P, CONV_W, CT])
        short_w = sb("short_w", [P, 4, 64])
        bias = sb("bias", [P, 72])
        eps = sb("eps", [P, 4])
        small = sb("small", [P, 2, 64])
        rms_c = sb("rms_c", [P, TT])
        rstd_c = sb("rstd_c", [P, TT])

        h1 = h_at + 32768
        qT = sb("qT", [P, HEADS0, T], at=h1)
        kT = sb("kT", [P, HEADS0, T], at=h1 + 8192)
        vT = sb("vT", [P, HEADS0, T], at=h1 + 16384)
        ncT = sb("ncT", [HEADS0, T], at=h1 + 24576)
        logf = sb("logf", [P, TT, HEADS0], at=h1 + 25600)
        cq = sb("cq", [P, TT, HEADS0], at=h1 + 25664)
        mx = sb("mx", [P, 2, TT], at=h1 + 25728)
        rsum = sb("rsum", [P, 2, TT], at=h1 + 25760)
        rinv = sb("rinv", [P, 2, TT], at=h1 + 25792)
        sp = [sb(f"sp{n}", [P, 64], at=h1 + 28672 + 256 * n) for n in range(8)]
        u_pad = sb("u_pad", [P, CT, CONV_W - 1 + T], at=h_at)
        u_sq = sb("u_sq", [P, CT, T], at=h_at)
        prod = sb("prod", [P, 2, CT - CONV_DVE, T], at=h_at + 16384)
        conv = sb("conv", [P, CT, T], at=xn_at)
        v_tok = sb("v_tok", [P, HEADS0, TT, P], at=x_at)
        sc = sb("sc", [P, 2, 2, T], at=x_at + 8192)
        pT = sb("pT", [P, 2, 384], at=x_at + 12288)
        stage = sb("stage", [P, TT, D], at=h1)
        vrow = sb("vrow", [P, 5, P], at=h_at)
        brow = sb("brow", [1, 72], at=h_at + 4096)
        wsm = sb("wsm", [P, KT, 64], at=h1 + 16384)
        wsm_s = sb("wsm_s", [P, KT, P], F32R, at=h1 + 20480)

        qk = sb("qk", [P, 2, SQ, T], at=h_at)
        qk_in = sb("qk_in", [P, 2, SQ, T], at=h_at + 8192)
        vs = sb("vs", [P, SV, T], at=h_at + 16384)
        zs = sb("zs", [P, SV, T], at=h_at + 24576)
        og = sb("og", [P, SV, T], at=h_at + 32768)
        slot_at = [h_at + 40960 + 2048 * n for n in range(12)] + [xn_at + 2048 * n for n in range(4)]
        slot = [[sb(f"slot{p}_{n}", [P, 4, P], at=slot_at[7 * p + n]) for n in range(7)] for p in range(2)]
        state = [sb(f"state{p}", [P, 2, P], at=slot_at[14] + 1024 * p) for p in range(2)]
        qk_sq = sb("qk_sq", [P, 2, SQ, T], at=slot_at[0])
        og_old = sb("og_old", [P, SV, T], at=slot_at[0])
        gate_b = sb("gate_b", [P, TT, V_HEADS])
        gate_g = sb("gate_g", [P, TT, V_HEADS])
        gate_c = sb("gate_c", [P, TT, V_HEADS])
        gate_ec = sb("gate_ec", [P, TT, V_HEADS], at=slot_at[15] + 0)
        gate_ed = sb("gate_ed", [P, TT, V_HEADS], at=slot_at[15] + 256)
        gate_bg = sb("gate_bg", [P, TT, V_HEADS], at=slot_at[15] + 512)
        gate_el = sb("gate_el", [P, 2 * TT, V_HEADS], at=slot_at[15] + 768)
        g_set = sb("g_set", [P, TT, SV])
        o_ss = sb("o_ss", [P, 2, 4])
        o_rs = sb("o_rs", [P, 2, 4])
        assert top[0] <= 212800, top[0]
        ctx.enter_context(nc.sbuf_tensor("arena", [P, top[0] // 4], F32))

        acc = ctx.enter_context(nc.psum_tensor("acc", [P, GM, GW], F32))
        aux = [ctx.enter_context(nc.psum_tensor(f"aux{n}", [P, 512], F32)) for n in range(4)]

        def sem(name):
            return ctx.enter_context(nc.semaphore(name))

        raw_in = [sem(f"raw_in{n}") for n in range(NCH)]
        hi_ready, lo_ready, w_used = sem("hi_ready"), sem("lo_ready"), sem("w_used")
        acc_ready, tmp_ready, acc_free = sem("acc_ready"), sem("tmp_ready"), sem("acc_free")
        const_in, x_in, const_step, const_pe, const_cp = (sem(n) for n in
            ("const_in", "x_in", "const_step", "const_pe", "const_cp"))
        x_trans, x_copied = sem("x_trans"), sem("x_copied")
        resid_added, sq_made, sq_added = sem("resid_added"), sem("sq_made"), sem("sq_added")
        ss_ready, rms_ready, rstd_ready = sem("ss_ready"), sem("rms_ready"), sem("rstd_ready")
        xn_ready, xsh_ready, xs_ready = sem("xn_ready"), sem("xsh_ready"), sem("xs_ready")
        gate_silu, h_prod, h_hi, h_ready = sem("gate_silu"), sem("h_prod"), sem("h_hi"), sem("h_ready")
        wsm_in, wsm_hi, wsm_lo, wsm_mm = [sem(f"wsm_in{n}") for n in range(2)], sem("wsm_hi"), sem("wsm_lo"), sem("wsm_mm")
        sp_dve, sp_act = sem("sp_dve"), sem("sp_act")
        fox_pe0, fox_cp = sem("fox_pe0"), sem("fox_cp")
        glu_sig, glu_made, conv_step = sem("glu_sig"), sem("glu_made"), sem("conv_step")
        conv_start, conv_act, conv_pool = sem("conv_start"), sem("conv_act"), sem("conv_pool")
        ln_pe, ln_dve, ln_act = sem("ln_pe"), sem("ln_dve"), sem("ln_act")
        vt_pe, vt_act = sem("vt_pe"), sem("vt_act")
        fx_pe = [sem(f"fx_pe{p}") for p in range(2)]
        fx_dve = [sem(f"fx_dve{p}") for p in range(2)]
        fx_act = [sem(f"fx_act{p}") for p in range(2)]
        fx_pool = [sem(f"fx_pool{p}") for p in range(2)]
        gg_pe, gg_dve, gg_act = sem("gg_pe"), sem("gg_dve"), sem("gg_act")
        sc_step, conv_silu = sem("sc_step"), sem("conv_silu")
        l2_act, l2_pe, l2_dve, gset_ready = sem("l2_act"), sem("l2_pe"), sem("l2_dve"), sem("gset_ready")
        gd_pe = [sem(f"gd_pe{p}") for p in range(2)]
        gd_dve = [sem(f"gd_dve{p}") for p in range(2)]
        gd_act = [sem(f"gd_act{p}") for p in range(2)]
        gd_pool = [sem(f"gd_pool{p}") for p in range(2)]
        pool_mark, act_mark = sem("pool_mark"), sem("act_mark")
        fg_tmp, fox_lf = sem("fg_tmp"), sem("fox_lf")
        og_saved, og_back, scaled = sem("og_saved"), sem("og_back"), sem("scaled")
        og_hi, og_ready, sq_zeroed = sem("og_hi"), sem("og_ready"), sem("sq_zeroed")
        y_made, y_pe, y_out, out_sent = sem("y_made"), sem("y_pe"), sem("y_out"), sem("out_sent")


        def rhs_of(g):
            return {"x": xs, "h0": hs[0], "h1": hs[1]}[g.rhs]

        def walk(eng, visit, peel_first=True):
            before = None
            for s in segs:
                last = len(s.groups) - 1

                def round_(i, before, end):
                    for b in range(last + 1):
                        kc = s.next_kc if end and b == last else s.groups[(b + 1) % (last + 1)].kc
                        here = Place(s, i, b)
                        visit(here, before, kc)
                        before = here
                lo = int(peel_first or s.first == 0)
                hi = s.n if s.next_kc == s.groups[0].kc else s.n - 1
                if lo:
                    round_(0, before, s.n == 1)
                if hi - lo == 1:
                    round_(lo, Place(s, lo - 1, last), lo == s.n - 1)
                elif hi > lo:
                    with eng.Fori(lo, hi) as i:
                        round_(i, Place(s, i - 1, last) if peel_first else None, False)
                if hi < s.n and s.n > lo:
                    round_(s.n - 1, Place(s, s.n - 2, last), True)
                before = Place(s, s.n - 1, last)
            return before

        def apart(pool):
            pool.sem_inc(pool_mark, 1)

        def set_of(here):
            return here.i if here.s.name == "in1" else SETS - 1

        def resid_no(here):
            return here.s.resid + (here.g.at if here.s.name == "in1_last" else here.i)

        def og_rows(j):
            return og_save[bass.ds(SV * P * j, SV * P), :].rearrange("(h p) t -> p h t", p=P)

        def rest(j, n):
            for _ in range(0 if isinstance(j, int) and j == SETS - 1 else n):
                yield

        def tick(steps, n=1):
            for _ in range(n):
                next(steps[0], None)

        def is_first(G):
            return isinstance(G, int) and G == 0

        def sync_program(sp_e):
            sp_e.dma_start(stage[:], x.rearrange("o (t p) d -> p (o t) d", p=P)).then_inc(x_in, 16)

            def load(here, before, kc):
                g, G = here.g, here.G
                w = weights[g.w]
                for c in range(NCH):
                    if not is_first(G):
                        sp_e.wait_ge(lo_ready, 8 * G + 2 * c - 6)
                    r0 = g.row + c * g.kc * P
                    col = bass.ds(g.col + g.step * here.i, GW)
                    sp_e.dma_start(raw[:, c, 0:g.kc], w[r0:r0 + g.kc * P, col].rearrange("(k p) n -> p k n", p=P))\
                        .then_inc(raw_in[c], 16)
            sp_e.wait_ge(const_in, 16 * 15)
            walk(sp_e, load, peel_first=False)
            for t in range(TT):
                sp_e.wait_ge(y_out, 15 + t)
                sp_e.dma_start(out[0, t * P:(t + 1) * P, :], stage[:, t]).then_inc(out_sent, 16)
            sp_e.wait_ge(out_sent, 16 * TT)

        def pool_program(pool):
            steps = [0]

            def link(ins):
                steps[0] += 1
                ins.then_inc(const_step, 1)
                pool.wait_ge(const_step, steps[0])

            def select(m, pattern, base_, mult, fill=0.0, op=ALU.is_ge):
                link(pool.affine_select(out=m, in_=m, compare_op=op, fill=fill, base=base_,
                                        pattern=pattern, channel_multiplier=mult))

            link(pool.memset(ident[:], 0.0))
            select(ident[:], [[-1, P]], 0, 1, fill=1.0, op=ALU.not_equal)
            link(pool.memset(ones[:], 1.0))
            link(pool.memset(triu[:], 1.0))
            select(triu[:], [[1, P]], 0, -1)
            link(pool.memset(chunk_triu[:], 1.0))
            select(chunk_triu[:], [[1, P]], 0, -1)
            select(chunk_triu[:, 64:P], [[0, 64]], -64, 1)
            link(pool.memset(chunk_ones[:], 1.0))
            select(chunk_ones[:, 64:P], [[0, 64]], -64, 1)
            select(chunk_ones[:, 0:64], [[0, 64]], 63, -1)
            link(pool.memset(mask_fox[:], 0.0))
            select(mask_fox[:], [[-1, P]], 0, 1, fill=NEG)
            link(pool.memset(mask_gdn[:], 0.0))
            select(mask_gdn[:], [[-1, P]], 0, 1, fill=NEG)
            select(mask_gdn[:, 0:64], [[0, 64]], 63, -1, fill=NEG)
            link(pool.memset(lvl[:], 0.0))
            for n in range(LEVELS):
                s = 1 << n
                upper = lvl[:, n, :].rearrange("p (b h w) -> p b h w", h=2, w=s)[:, :, 1, :]
                link(pool.memset(upper, 1.0))
                select(upper, [[-2 * s, P // (2 * s)], [0, s]], 0, 1)
                select(upper, [[2 * s, P // (2 * s)], [0, s]], s - 1, -1)
            link(pool.memset(lvl0t[:], 0.0))
            lower = lvl0t[:, :].rearrange("p (b h) -> p b h", h=2)[:, :, 0]
            link(pool.memset(lower, 1.0))
            select(lower, [[-2, P // 2]], -1, 1, fill=0.0, op=ALU.is_equal)
            for n, v in enumerate((EPS, P * EPS)):
                link(pool.memset(eps[:, n:n + 1], v))
            assert steps[0] == N_CONST, steps[0]
            pool.wait_ge(const_pe, 6)
            link(pool.memset(u_pad[:, :, 0:CONV_W - 1], 0.0))

            link(pool.memset(sq_acc[:], 0.0))
            for k in range(KT):
                pool.wait_ge(x_copied, k + 1)
                if k:
                    pool.wait_ge(sq_added, k)
                nc.gpsimd.tensor_tensor(sq_one[:], xT[:, k], xT[:, k], ALU.mult).then_inc(sq_made, 1)
                pool.wait_ge(sq_made, k + 1)
                nc.gpsimd.tensor_tensor(sq_acc[:], sq_acc[:], sq_one[:], ALU.add).then_inc(sq_added, 1)

            def resid_row(here, m):
                t0 = 4 * (here.g.at if here.s.name == "in1_last" else here.i)
                return xT[:, bass.ds(t0 + m, 1), :].rearrange("p a t -> p (a t)")

            def post(here):
                s, i, g, G = here.s, here.i, here.g, here.G
                if g.kind == "resid":
                    R = resid_no(here)
                    for m in range(GM):
                        pool.wait_ge(acc_free, 4 * G + m + 1)
                        apart(pool)
                        row = resid_row(here, m)
                        nc.gpsimd.tensor_tensor(row, row, ut[:, m], ALU.add).then_inc(resid_added, 1)
                    if g.norm is not None:
                        for m in range(GM):
                            n = 16 * g.norm + 4 * i + m
                            pool.wait_ge(resid_added, 4 * R + m + 1)
                            pool.wait_ge(sq_added, n)
                            apart(pool)
                            row = resid_row(here, m)
                            nc.gpsimd.tensor_tensor(sq_one[:], row, row, ALU.mult).then_inc(sq_made, 1)
                            pool.wait_ge(sq_made, n + 1)
                            nc.gpsimd.tensor_tensor(sq_acc[:], sq_acc[:], sq_one[:], ALU.add).then_inc(sq_added, 1)
                if g.kind == "glu_gate":
                    pool.wait_ge(glu_sig, i + 1)
                    nc.gpsimd.tensor_tensor(u_pad[:, 4 * i:4 * i + 4, CONV_W - 1:], gt[:], ut[:],
                                            ALU.mult).then_inc(glu_made, 1)
                if g.kind == "up":
                    q = s.pair + i
                    pool.wait_ge(gate_silu, q + 1)
                    pool.wait_ge(scaled, here.scaled + 1)
                    nc.gpsimd.tensor_tensor(ut[:], gt[:], ut[:], ALU.mult).then_inc(h_prod, 1)
                    pool.wait_ge(h_prod, q + 1)
                    apart(pool)
                    hb = hs[g.at % 2]
                    hi = hb[:, bass.ds(4 * i, 4), 0, :]
                    nc.gpsimd.tensor_copy(hi, ut[:]).then_inc(h_hi, 1)
                    pool.wait_ge(h_hi, q + 1)
                    apart(pool)
                    nc.gpsimd.tensor_tensor(hb[:, bass.ds(4 * i, 4), 1, :], ut[:], hi.bitcast(F32),
                                            ALU.subtract).then_inc(h_ready, 1)

            steps = [iter(())]

            def visit(here, before, kc):
                s, i, b, g = here.s, here.i, here.b, here.g
                if s.name == "out0" and here.starts:
                    fox_pool(pool)
                    before = None
                if before is not None:
                    post(before)
                if s.name == "qkv" and here.starts:
                    conv_taps_pool(pool)
                if here.starts and g.kind == "resid" and g.norm is not None:
                    pool.wait_ge(ss_ready, g.norm)
                    pool.memset(sq_acc[:], 0.0).then_inc(sq_zeroed, 1)
                    pool.wait_ge(sq_zeroed, g.norm)
                if s.name == "down2" and s.resid < 16 and here.starts:
                    pool.wait_ge(acc_ready, 4 * s.first)
                    pool.dma_start(wsm[:], w_in1[0, :, BA_COL:BA_COL + 64]
                                   .rearrange("(k p) n -> p k n", p=P)).then_inc(wsm_in[1], 16)
                if s.deltanet:
                    if b == 0:
                        steps[0] = gdn_pool(pool, set_of(here))
                    if s.name == "in1_last" and b == 2:
                        pool.wait_ge(l2_dve, 2 * SETS)
                        pool.dma_start(qk_in[:].rearrange("p a b t -> p (a b) t"), og_rows(0)).then_inc(og_back, 16)
                    for c in range(NCH):
                        tick(steps, 6)
                        if s.name == "in1_last" and b == 2 and c == 0:
                            pool.wait_ge(og_ready, 2)
                            pool.dma_start(qk_in[:].rearrange("p a b t -> p (a b) t"), og_rows(1)).then_inc(og_back, 16)
                    if b == len(s.groups) - 1:
                        for _ in steps[0]:
                            pass
                        if s.name == "in1_last":
                            pool.dma_start(og_old[:], og_rows(2)).then_inc(og_back, 16)
            walk(pool, visit)

        def scalar_program(act):
            def split_hi(G, c, kc, h):
                act.wait_ge(raw_in[c], 16 * G + 16)
                if not (isinstance(G, int) and G == 0 and c < 2):
                    if c == 1:
                        act.wait_ge(acc_ready, 4 * G)
                    else:
                        act.wait_ge(w_used, 3 * G + (c - 1 if c else 0))
                k = slice(0, 2) if h == 0 else slice(2, kc)
                nc.scalar.activation(w_hi[:, c % 2, k], raw[:, c, k], ACT.Copy).then_inc(hi_ready, 1)

            def sums(G, m):
                act.wait_ge(acc_ready, 4 * G + m + 1)
                if not (is_first(G) and m < 2):
                    act.wait_ge(acc_free, 4 * G + m - 1)
                nc.scalar.activation(tmp[:, m % 2], acc[:, m, T:2 * T], ACT.Copy).then_inc(tmp_ready, 1)

            def post(here):
                s, i, g, G = here.s, here.i, here.g, here.G
                if g.kind == "gate":
                    act.wait_ge(scaled, here.scaled + 1)
                    nc.scalar.activation(gt[:], gt[:], ACT.Silu).then_inc(gate_silu, 1)
                if g.kind == "glu_gate":
                    act.wait_ge(scaled, here.scaled + 1)
                    nc.scalar.activation(gt[:], gt[:], ACT.Sigmoid).then_inc(glu_sig, 1)
                if g.kind == "resid" and g.norm in (1, 2, 3):
                    n = 4 * g.norm + i
                    act.wait_ge(xn_ready, n + 1)
                    act_apart(act)
                    nc.scalar.activation(xs[:, bass.ds(4 * i, 4), 0, :], xn[:, 0], ACT.Copy).then_inc(xsh_ready, 1)

            def og_upper(c0, count, src):
                for c in range(c0, c0 + count):
                    k = 4 * (c % 4)
                    dst = xs if c < 4 else hs[0]
                    a = 4 * (c % 2)
                    nc.scalar.activation(dst[:, k:k + 4, 0, :], src[:, a:a + 4], ACT.Copy).then_inc(og_hi, 1)

            rows = [(norm_mix0, G_MIX0, 16), (norm_mix1, G_MIX1, 16), (norm_ffn, G_FFN0, 32),
                    (final_norm, G_FINAL, 16), (conv_b0, CB, 8), (conv_ln_g0, LG, 8), (conv_ln_b0, LB, 8),
                    (o_norm1, ON, 1)]
            for src, r, n in rows:
                flat = src if len(src.shape) == 1 else src.rearrange("a b -> (a b)")
                act.dma_start(vrow[r:r + n, 0, :], flat.rearrange("(a b) -> a b", b=P)).then_inc(const_in, 16)
            cw = conv_w0[0].rearrange("w (c p) -> (w c) p", p=P)
            act.dma_start(vrow[0:124, 1, :], cw[0:124]).then_inc(const_in, 16)
            act.dma_start(vrow[0:124, 2, :], cw[124:248]).then_inc(const_in, 16)
            sw = short_conv1[0].rearrange("w (c p) -> (w c) p", p=P)
            act.dma_start(vrow[:, 3, :], sw[0:128]).then_inc(const_in, 16)
            act.dma_start(vrow[:, 4, :], sw[128:256]).then_inc(const_in, 16)
            act.dma_start(brow[:, 0:8], fgate_bias0).then_inc(const_in, 16)
            act.dma_start(brow[:, 8:40], a_log1).then_inc(const_in, 16)
            act.dma_start(brow[:, 40:72], dt_bias1).then_inc(const_in, 16)
            act.dma_start(wsm[:, :, 0:HEADS0], w_in0[0, :, F_COL:F_COL + HEADS0]
                           .rearrange("(k p) n -> p k n", p=P)).then_inc(wsm_in[0], 16)
            act.wait_ge(const_pe, 6)
            nc.scalar.activation(vec[:], aux[0][:, 0:NVEC], ACT.Copy).then_inc(const_cp, 1)
            nc.scalar.activation(conv_w[:].rearrange("p w c -> p (w c)"), aux[1][:, 0:248], ACT.Copy).then_inc(const_cp, 1)
            nc.scalar.activation(short_w[:].rearrange("p w c -> p (w c)"), aux[2][:, 0:256], ACT.Copy).then_inc(const_cp, 1)
            nc.scalar.activation(bias[:], aux[3][:, 0:72], ACT.Copy).then_inc(const_cp, 1)
            for k in range(0, KT, 2):
                act.wait_ge(x_trans, k // 2 + 1)
                for h in range(2):
                    nc.scalar.activation(xT[:, k + h], acc[:, (k // 2) % 4, h * T:(h + 1) * T], ACT.Copy)\
                        .then_inc(x_copied, 1)
            act.wait_ge(const_step, N_CONST)
            for c in range(4):
                act.wait_ge(xn_ready, c + 1)
                nc.scalar.activation(xs[:, 4 * c:4 * c + 4, 0, :], xn[:, c % 2], ACT.Copy).then_inc(xsh_ready, 1)
            split_hi(0, 0, 4, 0)
            split_hi(0, 0, 4, 1)
            steps = [iter(())]

            def visit(here, before, kc):
                s, i, b, g, G = here.s, here.i, here.b, here.g, here.G
                if s.name == "out0" and here.starts:
                    post(before)
                    before = None
                    ln_act_steps(act)
                    fox_act(act)
                if s.deltanet and b == 0:
                    steps[0] = gdn_act(act, set_of(here))
                qk_old = qk_in[:].rearrange("p a b t -> p (a b) t")
                if s.name == "in1_last" and b == 2:
                    act.wait_ge(og_back, 16)
                    act.wait_ge(acc_ready, 4 * G)
                    og_upper(0, 2, qk_old)
                if s.name == "out1b" and here.starts:
                    for p in range(2):
                        act.wait_ge(gd_dve[p], ND * 2 * SETS)
                        act.wait_ge(gd_pe[p], NP * 2 * SETS)
                    act.wait_ge(og_back, 48)
                    og_upper(4, 2, og_old)
                    og_upper(6, 2, og)
                for c in range(NCH):
                    def split(h):
                        if c < NCH - 1:
                            split_hi(G, c + 1, g.kc, h)
                        elif kc:
                            split_hi(G + 1, 0, kc, h)

                    split(0)
                    tick(steps, 2 if s.deltanet and c < NCH - 1 else 0)
                    if c < NCH - 1 or not s.deltanet:
                        split(1)
                    if s.name == "in1_last" and b == 2 and c == 1:
                        act.wait_ge(og_back, 32)
                        og_upper(2, 2, qk_old)
                    if c == 0 and before is not None:
                        post(before)
                    if here.starts and c == 1 and g.norm is not None and g.kind != "resid" and s.name in NORMED:
                        norm_act(act, g.norm)
                    narrow_act(act, here, c)
                    if s.name == "qkv":
                        conv_taps_act(act, 12 * i + 4 * b + c - 1)
                    if c < NCH - 1:
                        tick(steps, 4 if s.deltanet else 0)
                    else:
                        in_turn(steps, s.deltanet, lambda m: sums(G, m), split)
                    if c == 2 and before is not None and before.g.kind.startswith("gdn"):
                        silu_act(act, before)
                if s.deltanet and b == len(s.groups) - 1:
                    for _ in steps[0]:
                        pass
            walk(act, visit)
            norm_act(act, 4)
            for k in range(KT // 2):
                act.wait_ge(y_pe, k + 1)
                for t in range(TT):
                    nc.scalar.activation(stage[:, t, k * T:(k + 1) * T], aux[(2 * k + t) % 4][:, 0:T], ACT.Copy)\
                        .then_inc(y_out, 1)

        def in_turn(steps, on, sum_, split):
            for n, m in enumerate((0, None, 1, None, 2, 3)):
                if on and n in (0, 1, 3, 4):
                    tick(steps)
                if m is not None:
                    sum_(m)
                if on and n in (2, 5):
                    tick(steps)
                if on and n == 1:
                    split(1)

        def act_apart(act):
            act.sem_inc(act_mark, 1)

        def silu_act(act, here):
            kind = here.g.kind
            if here.b in here.s.conv_of:
                act.wait_ge(sc_step, 8 * here.conv + 8)
            else:
                act.wait_ge(scaled, here.scaled + 1)
            if here.s.name == "in1" and kind in ("gdn_q", "gdn_k"):
                act.wait_ge(l2_dve, 2 * here.i + 2)
            if here.s.name == "in1" and kind == "gdn_v0":
                for p in range(2):
                    act.wait_ge(gd_pe[p], NP * (2 * here.i + 1) + P_KT)
            dst = {"gdn_q": qk_in[:, 0], "gdn_k": qk_in[:, 1], "gdn_v0": vs[:, 0:4], "gdn_v1": vs[:, 4:8],
                   "gdn_z0": zs[:, 0:4], "gdn_z1": zs[:, 4:8]}[kind]
            src = gt if here.b in here.s.conv_of else ut
            nc.scalar.activation(dst, src[:], ACT.Silu).then_inc(conv_silu, 1)

        def norm_act(act, n):
            act.wait_ge(ss_ready, n + 1)
            nc.scalar.activation(rms[:], aux[0][:, 0:T], ACT.Sqrt, bias=eps[:, 0:1], scale=1.0 / D).then_inc(rms_ready, 1)
            nc.scalar.activation(rms_c[:], aux[0][:, T:T + TT], ACT.Sqrt, bias=eps[:, 0:1], scale=1.0 / D)\
                .then_inc(rms_ready, 1)

        def narrow_act(act, here, c):
            n = here.G - here.s.first
            if here.s.name == "glu":
                if (n, c) == (0, 2):
                    small_act(act, 0, HEADS0)
                if (n, c) == (1, 1):
                    softplus_act(act, 0)
                if (n, c) == (2, 1):
                    fox_gate_act(act)
            if here.s.name == "in1_first":
                if (n, c) == (0, 2):
                    small_act(act, 1, 64)
                if (n, c) == (1, 1):
                    gates_act1(act)
                if (n, c) == (2, 1):
                    gates_act2(act)

        def small_act(act, which, n):
            act.wait_ge(wsm_in[which], 16)
            nc.scalar.activation(wsm_s[:, :, 0:n], wsm[:, :, 0:n], ACT.Copy).then_inc(wsm_hi, 1)

        def softplus_act(act, n):
            act.wait_ge(sp_dve, SPD * n + 3)
            nc.scalar.activation(sp[2][:], sp[1][:], ACT.Exp, scale=-1.0).then_inc(sp_act, 1)
            act.wait_ge(sp_dve, SPD * n + 4)
            nc.scalar.activation(sp[4][:], sp[3][:], ACT.Ln).then_inc(sp_act, 1)

        def fox_gate_act(act):
            act.wait_ge(fox_pe0, 1)
            nc.scalar.activation(ncT[:], aux[1][0:HEADS0, 0:T], ACT.Copy, scale=-math.sqrt(P)).then_inc(fox_cp, 1)
            nc.scalar.activation(cq[:].rearrange("p t h -> p (t h)"), aux[2][:, 0:16], ACT.Copy).then_inc(fox_cp, 1)

        def ln_act_steps(act):
            for h in range(HEADS0):
                if h == HEADS0 // 2:
                    act.wait_ge(ln_dve, 1)
                    nc.scalar.activation(u_sq[:], conv[:], ACT.Square).then_inc(ln_act, 1)
                act.wait_ge(vt_pe, h + 1)
                nc.scalar.activation(v_tok[:, h], aux[2 + h % 2][:, 0:T], ACT.Copy).then_inc(vt_act, 1)
            act.wait_ge(ln_pe, 2)
            nc.scalar.activation(rms[:], aux[1][:, 0:T], ACT.Sqrt, bias=eps[:, 0:1], scale=1.0 / 1024).then_inc(ln_act, 1)
            act.wait_ge(ln_dve, 3)
            for c in range(CT):
                last = nc.scalar.activation(u_sq[:, c], conv[:, c], ACT.Silu, scale=vec[:, LG + c:LG + c + 1],
                                            bias=vec[:, LB + c:LB + c + 1])
            last.then_inc(ln_act, 1)
            act.wait_ge(ln_act, 3)
            nc.scalar.activation(hs[0][:, 8:16, 0, :], u_sq[:], ACT.Copy).then_inc(ln_act, 1)

        def fox_act(act):
            for n in range(HEADS0 // 2):
                for p in range(2):
                    act.wait_ge(fx_dve[p], FOX_MAX(n))
                    for t in range(TT):
                        w = sc[:, p, t, 0:P * (t + 1)]
                        nc.scalar.activation(w, w, ACT.Exp, bias=mx[:, p, t:t + 1], accum_out=rsum[:, p, t:t + 1])\
                            .then_inc(fx_act[p], 1)
                for p in range(2):
                    act.wait_ge(fx_pe[p], FOX_TR(n))
                    nc.scalar.activation(pT[:, p], aux[2 * p + 1][:, 0:384], ACT.Copy).then_inc(fx_act[p], 1)
                for p in range(2):
                    act.wait_ge(fx_pe[p], FOX_AV(n))
                    act.wait_ge(ln_dve, 4)
                    nc.scalar.activation(hs[0][:, 2 * n + p, 0, :], aux[2 * p + 1][:, 0:T], ACT.Copy)\
                        .then_inc(fx_act[p], 1)

        def gates_act1(act):
            act.wait_ge(gg_dve, 1)
            nc.scalar.activation(gate_b[:], small[:, :, 0:32], ACT.Sigmoid).then_inc(gg_act, 1)
            softplus_act(act, 1)
            act.wait_ge(gg_act, 1)
            nc.scalar.activation(small[:, 0, 0:32], bias[:, 8:40], ACT.Exp).then_inc(gg_act, 1)

        def gates_act2(act):
            act.wait_ge(gg_pe, 1)
            nc.scalar.activation(gate_c[:].rearrange("p t h -> p (t h)"), aux[1][:, 0:64], ACT.Copy).then_inc(gg_act, 1)
            nc.scalar.activation(gate_ec[:].rearrange("p t h -> p (t h)"), aux[1][:, 0:64], ACT.Exp).then_inc(gg_act, 1)
            act.wait_ge(gg_pe, 2)
            nc.scalar.activation(gate_el[:].rearrange("p c h -> p (c h)"), aux[3][:, 0:128], ACT.Exp).then_inc(gg_act, 1)
            act.wait_ge(gg_dve, 4)
            nc.scalar.activation(gate_ed[:], gate_ed[:], ACT.Exp).then_inc(gg_act, 1)

        def gdn_act(act, j):
            act.wait_ge(gg_act, 6)
            act.wait_ge(conv_silu, K_SILU + 6 * j)
            nc.scalar.activation(qk_sq[:], qk_in[:], ACT.Square).then_inc(l2_act, 1)
            for _ in range(5):
                yield
            act.wait_ge(l2_pe, j + 1)
            for n in range(4):
                q = n < 2
                nc.scalar.activation(qk_sq[:, n // 2, 2 * (n % 2):2 * (n % 2) + 2, :].rearrange("p a t -> p (a t)"),
                                     aux[n][:], ACT.Ln, bias=eps[:, 1:2] if q else eps[:, 0:1],
                                     scale=float(P) if q else 1.0).then_inc(l2_act, 1)
            act.wait_ge(l2_act, 6 * j + 5)
            nc.scalar.activation(qk_sq[:], qk_sq[:], ACT.Exp, scale=-0.5).then_inc(l2_act, 1)
            for _ in range(PRELUDE - 5):
                yield
            for u in range(2):
                yield from gdn_act_steps(act, j, u)
            for p in range(2):
                act.wait_ge(gd_dve[p], ND * (2 * j + 2))

        def flat(t):
            return t.rearrange("p a b -> p (a b)")

        def gdn_act_steps(act, j, u):
            n = 2 * j + u
            yield from rest(j, 1)
            for p in range(2):
                s0 = slot[p][0]
                act.wait_ge(gd_pool[p], NO * n + O_MASK)
                nc.scalar.activation(s0[:], s0[:], ACT.Exp).then_inc(gd_act[p], 1)
                yield
            yield from rest(j, 3)
            yield
            yield
            for p in range(2):
                act.wait_ge(gd_pe[p], NP * n + P_LT)
                nc.scalar.activation(flat(slot[p][4][:]), aux[2 * p][:], ACT.Copy).then_inc(gd_act[p], 1)
                act.wait_ge(gd_pe[p], NP * n + P_IT)
                nc.scalar.activation(flat(slot[p][3][:]), aux[2 * p + 1][:], ACT.Copy).then_inc(gd_act[p], 1)
                yield
            yield
            yield
            for lv in range(1, LEVELS):
                for p in range(2):
                    act.wait_ge(gd_pe[p], NP * n + P_LV(lv, 0))
                    nc.scalar.activation(flat(slot[p][2][:]), aux[2 * p][:], ACT.Copy).then_inc(gd_act[p], 1)
                    yield
                yield
                yield
                if lv < LEVELS - 1:
                    for p in range(2):
                        act.wait_ge(gd_pe[p], NP * n + P_LV(lv, 2))
                        nc.scalar.activation(flat(slot[p][6][:]), aux[2 * p][:], ACT.Copy).then_inc(gd_act[p], 1)
                        yield
            yield
            yield
            for p in range(2):
                act.wait_ge(gd_pe[p], NP * n + P_U)
                nc.scalar.activation(flat(slot[p][4][:]), aux[2 * p][:], ACT.Copy).then_inc(gd_act[p], 1)
                act.wait_ge(gd_pe[p], NP * n + P_W)
                nc.scalar.activation(flat(slot[p][5][:]), aux[2 * p + 1][:], ACT.Copy).then_inc(gd_act[p], 1)
                yield
            yield
            yield
            for c in range(1, 4):
                t, r = c // 2, slice(64 * (c % 2), 64 * (c % 2) + 64)
                for p in range(2):
                    a = 2 * u + p
                    act.wait_ge(gd_dve[p], ND * n + D_VN(c))
                    for b in range(2):
                        nc.scalar.activation(slot[p][1][r, 2 * b + t, :], aux[2 * p][r, (2 + b) * P:(3 + b) * P], ACT.Copy,
                                             scale=gate_ec[r, t, bass.ds(SV * j + 2 * a + b, 1)]).then_inc(gd_act[p], 1)
                    yield
                if c < 3:
                    yield
                    yield
            yield
            yield
            yield from rest(j, 1)
            for p in range(2):
                act.wait_ge(gd_dve[p], ND * n + D_SS)
                nc.scalar.activation(o_rs[:, p], o_ss[:, p], ACT.Sqrt, bias=eps[:, 0:1], scale=1.0 / P)\
                    .then_inc(gd_act[p], 1)
                yield
            yield
            yield
            yield

        def vector_program(dve):
            def split_lo(G, c, kc, h):
                dve.wait_ge(hi_ready, 8 * G + 2 * c + h + 1)
                k = slice(0, 2) if h == 0 else slice(2, kc)
                nc.vector.tensor_tensor(w_lo[:, c % 2, k], raw[:, c, k], w_hi[:, c % 2, k].bitcast(F32),
                                        ALU.subtract).then_inc(lo_ready, 1)

            def sums(here, m, dst):
                dve.wait_ge(tmp_ready, 4 * here.G + m + 1)
                nc.vector.tensor_tensor(dst, acc[:, m, 0:T], tmp[:, m % 2], ALU.add).then_inc(acc_free, 1)

            def fox_tiles(here):
                return (qT, kT, vT)[int(here.g.kind[3])][:, 4 * here.i:4 * here.i + 4]

            def room(here, before):
                s, i, b, kind = here.s, here.i, here.b, here.g.kind
                if kind == "resid":
                    if not (isinstance(here.i, int) and resid_no(here) == 0):
                        dve.wait_ge(resid_added, 4 * resid_no(here))
                    if s.pair:
                        dve.wait_ge(h_ready, s.pair)
                    if s.name == "in1_last":
                        dve.wait_ge(conv_silu, s.silu + 2)
                elif kind == "gate":
                    if not (isinstance(i, int) and i + s.pair == 0):
                        dve.wait_ge(h_prod, s.pair + i)
                elif kind == "up":
                    if not (isinstance(i, int) and i + s.pair == 0):
                        dve.wait_ge(h_ready, s.pair + i)
                    dve.wait_ge(resid_added, 4 * s.resid)
                elif kind == "glu_val" and i:
                    dve.wait_ge(glu_made, i)
                elif kind.startswith("gdn"):
                    dve.wait_ge(resid_added, 4 * s.resid)
                    if before is not None and before.g.kind.startswith("gdn"):
                        dve.wait_ge(conv_silu, before.silu + 1)

            def place(here):
                kind = here.g.kind
                if kind.startswith("fox"):
                    return fox_tiles(here)
                return gt[:] if kind in ("gate", "glu_gate") else ut[:]

            def gain_split(n, i):
                for k in range(4):
                    kt = 4 * i + k
                    last = nc.vector.tensor_scalar(xn[:, 0, k],
                                                   xT[:, bass.ds(kt, 1), :].rearrange("p a t -> p (a t)"),
                                                   vec[:, bass.ds(NORM_COL[n] + kt, 1)], None, ALU.mult)
                last.then_inc(xn_ready, 1)
                dve.wait_ge(xsh_ready, 4 * n + i + 1)
                nc.vector.tensor_tensor(xs[:, bass.ds(4 * i, 4), 1, :], xn[:, 0],
                                        xs[:, bass.ds(4 * i, 4), 0, :].bitcast(F32), ALU.subtract).then_inc(xs_ready, 1)

            def post(here):
                g = here.g
                if g.kind == "resid":
                    if g.norm in (1, 2, 3):
                        dve.wait_ge(resid_added, 4 * resid_no(here) + 4)
                        dve.wait_ge(xs_ready, 4 * g.norm + here.i)
                        gain_split(g.norm, here.i)
                    return
                dve.wait_ge(acc_free, 4 * here.G + 4)
                dst = place(here)
                nc.vector.tensor_tensor(dst, dst, rstd[:].unsqueeze(1).to_broadcast([P, 4, T]), ALU.mult)\
                    .then_inc(scaled, 1)

            def og_lower(c0, count, src):
                for c in range(c0, c0 + count):
                    k, a = 4 * (c % 4), 4 * (c % 2)
                    dst = xs if c < 4 else hs[0]
                    dve.wait_ge(og_hi, c + 1)
                    nc.vector.tensor_tensor(dst[:, k:k + 4, 1, :], src[:, a:a + 4], dst[:, k:k + 4, 0, :].bitcast(F32),
                                            ALU.subtract).then_inc(og_ready, 1)

            def conv_step_of(here, q):
                s = q // 2
                n0 = 4 * here.conv
                i, b = here.i, here.b - here.s.conv_of[0]
                j = i + 1 if here.s.name == "in1" else 0
                ct = (4 * j, 16 + 4 * j, 32 + 8 * j, 36 + 8 * j)[b]
                if s:
                    dve.wait_ge(sc_step, 2 * n0 + q - 1)
                else:
                    dve.wait_ge(scaled, here.scaled + 1)
                for m in range(2 * (q % 2), 2 * (q % 2) + 2):
                    w = short_w[:, 3 - s, bass.ds(ct + m, 1)]
                    if s == 0:
                        last = nc.vector.tensor_scalar(gt[:, m], ut[:, m], w, None, ALU.mult)
                    else:
                        last = nc.vector.scalar_tensor_tensor(gt[:, m, s:T], ut[:, m, 0:T - s], w, gt[:, m, s:T],
                                                              ALU.mult, ALU.add)
                last.then_inc(sc_step, 1)

            dve.wait_ge(const_step, N_CONST)
            dve.wait_ge(const_cp, 4)
            dve.wait_ge(x_copied, KT)
            for c in range(4):
                if c >= 2:
                    dve.wait_ge(xs_ready, c - 1)
                for k in range(4):
                    kt = 4 * c + k
                    last = nc.vector.tensor_scalar(xn[:, c % 2, k], xT[:, kt], vec[:, G_MIX0 + kt:G_MIX0 + kt + 1], None,
                                                   ALU.mult)
                last.then_inc(xn_ready, 1)
                if c >= 1:
                    first_lower(dve, c - 1)
            first_lower(dve, 3)
            split_lo(0, 0, 4, 0)
            split_lo(0, 0, 4, 1)
            steps = [iter(())]

            def visit(here, before, kc):
                s, i, b, g, G = here.s, here.i, here.b, here.g, here.G
                if s.name == "out0" and here.starts:
                    post(before)
                    before = None
                    ln_dve_steps(dve)
                    fox_dve(dve)
                if s.deltanet and b == 0:
                    steps[0] = gdn_dve(dve, set_of(here))
                qk_old = qk_in[:].rearrange("p a b t -> p (a b) t")
                if s.name == "in1_last" and b == 2:
                    og_lower(0, 2, qk_old)
                if s.name == "out1b" and here.starts:
                    og_lower(4, 2, og_old)
                    og_lower(6, 2, og)
                taps = before is not None and before.b in before.s.conv_of
                for c in range(NCH):
                    def split(h):
                        if c < NCH - 1:
                            split_lo(G, c + 1, g.kc, h)
                        elif kc:
                            split_lo(G + 1, 0, kc, h)

                    on = s.deltanet
                    tick(steps, 1 if on and c < NCH - 1 else 0)
                    split(0)
                    tick(steps, 1 if on and c < NCH - 1 else 0)
                    if c < NCH - 1 or not on:
                        split(1)
                    if s.name == "in1_last" and b == 2 and c == 1:
                        og_lower(2, 2, qk_old)
                    if c == 0 and before is not None:
                        post(before)
                    if here.starts and c == 1 and s.name in NORMED:
                        norm_dve(dve, g.norm)
                    narrow_dve(dve, here, c)
                    if s.name == "qkv":
                        conv_taps_dve(dve, 12 * i + 4 * b + c - 1)
                    if c < NCH - 1:
                        for h in range(4):
                            q = 4 * c + h - 2
                            tick(steps, 1 if on else 0)
                            if taps and 0 <= q < 8:
                                conv_step_of(before, q)
                    else:
                        room(here, before)
                        dst = place(here)
                        in_turn(steps, on, lambda m: sums(here, m, dst[:, m]), split)
                if s.deltanet and b == len(s.groups) - 1:
                    for _ in steps[0]:
                        pass
            here = walk(dve, visit)
            R, i = resid_no(here), here.i
            dve.wait_ge(sq_added, 16 * 4 + 4 * i)
            for m in range(GM):
                row = xT[:, 4 * i + m]
                dve.wait_ge(acc_free, 4 * here.G + m + 1)
                nc.vector.tensor_tensor(row, row, ut[:, m], ALU.add).then_inc(resid_added, 1)
            for m in range(GM):
                row, n = xT[:, 4 * i + m], 16 * 4 + 4 * i + m
                one = tmp[:, m % 2]
                dve.wait_ge(resid_added, 4 * R + m + 1)
                nc.vector.tensor_tensor(one, row, row, ALU.mult).then_inc(sq_made, 1)
                dve.wait_ge(sq_made, n + 1)
                dve.wait_ge(sq_added, n)
                nc.vector.tensor_tensor(sq_acc[:], sq_acc[:], one, ALU.add).then_inc(sq_added, 1)
            norm_dve(dve, 4)
            for c in range(4):
                for k in range(4):
                    kt = 4 * c + k
                    last = nc.vector.scalar_tensor_tensor(xT[:, kt], xT[:, kt], vec[:, G_FINAL + kt:G_FINAL + kt + 1],
                                                          rstd[:], ALU.mult, ALU.mult)
                last.then_inc(y_made, 1)

        def first_lower(dve, c):
            dve.wait_ge(xsh_ready, c + 1)
            nc.vector.tensor_tensor(xs[:, 4 * c:4 * c + 4, 1, :], xn[:, c % 2],
                                    xs[:, 4 * c:4 * c + 4, 0, :].bitcast(F32), ALU.subtract).then_inc(xs_ready, 1)

        def norm_dve(dve, n):
            dve.wait_ge(rms_ready, 2 * n + 2)
            nc.vector.reciprocal(rstd[:], rms[:]).then_inc(rstd_ready, 1)
            nc.vector.reciprocal(rstd_c[:], rms_c[:]).then_inc(rstd_ready, 1)
            dve.wait_ge(rstd_ready, 2 * n + 2)

        def narrow_dve(dve, here, c):
            n = here.G - here.s.first
            if here.s.name == "glu":
                if (n, c) == (0, 2):
                    small_lower(dve, 0, HEADS0)
                if (n, c) == (1, 1):
                    small_dve(dve, 0, HEADS0)
                    fox_gate_dve(dve)
            if here.s.name == "in1_first":
                if (n, c) == (0, 2):
                    small_lower(dve, 1, 64)
                if (n, c) == (1, 1):
                    small_dve(dve, 1, 64)
                    gates_dve1(dve)
                if (n, c) == (2, 1):
                    gates_dve2(dve)

        def small_lower(dve, which, n):
            dve.wait_ge(wsm_hi, which + 1)
            nc.vector.tensor_tensor(wsm_s[:, :, n:2 * n], wsm[:, :, 0:n], wsm_s[:, :, 0:n].bitcast(F32), ALU.subtract)\
                .then_inc(wsm_lo, 1)

        def small_dve(dve, which, n):
            dve.wait_ge(wsm_mm, which + 1)
            ps = aux[3][:, 0:4 * n].rearrange("p (t two n) -> p t two n", t=TT, two=2)
            nc.vector.tensor_copy(small[:, :, 0:n], ps[:, :, 1]).then_inc(sp_dve, 1)
            dve.wait_ge(sp_dve, SPD * which + 1)

        def fox_gate_dve(dve):
            z, az, e, u, ln, d, m, r = (t[:] for t in sp)
            w = TT * HEADS0
            ps = aux[3][:, 0:4 * HEADS0].rearrange("p (t two n) -> p t two n", t=TT, two=2)
            s0 = small[:, :, 0:HEADS0]
            steps = [1]

            def link(ins):
                steps[0] += 1
                ins.then_inc(sp_dve, 1)
                dve.wait_ge(sp_dve, steps[0])

            def w2(t):
                return t[:, 0:w].rearrange("p (t h) -> p t h", t=TT)
            fb = bias[:, 0:HEADS0].unsqueeze(1).to_broadcast([P, TT, HEADS0])
            nc.vector.memset(az, 0.0)
            nc.vector.memset(u, 1.0)
            nc.vector.memset(z, 0.0)
            nc.vector.tensor_tensor(s0, ps[:, :, 0], s0, ALU.add).then_inc(fg_tmp, 1)
            dve.wait_ge(fg_tmp, 1)
            nc.vector.tensor_tensor(s0, s0, rstd_c[:].unsqueeze(2).to_broadcast([P, TT, HEADS0]), ALU.mult).then_inc(fg_tmp, 1)
            dve.wait_ge(fg_tmp, 2)
            nc.vector.tensor_tensor(s0, s0, fb, ALU.add).then_inc(fg_tmp, 1)
            dve.wait_ge(fg_tmp, 3)
            link(nc.vector.tensor_scalar(w2(z), s0, -1.0, None, ALU.mult))
            softplus_steps(dve, link, z, az, e, u, ln, d, m, r, 0, s0, None)
            nc.vector.tensor_scalar(logf[:], w2(ln), -1.0, None, ALU.mult).then_inc(fox_lf, 1)

        def softplus_steps(dve, link, z, az, e, u, ln, d, m, r, which, s0, _):
            link(nc.vector.scalar_tensor_tensor(az, z, -1.0, z, ALU.mult, ALU.max))
            dve.wait_ge(sp_act, 2 * which + 1)
            link(nc.vector.tensor_scalar(u, e, 1.0, None, ALU.add))
            link(nc.vector.tensor_scalar(d, u, -1.0, None, ALU.add))
            link(nc.vector.tensor_scalar(m, d, 0.0, None, ALU.is_equal))
            link(nc.vector.tensor_tensor(d, d, m, ALU.add))
            link(nc.vector.reciprocal(r, d))
            dve.wait_ge(sp_act, 2 * which + 2)
            link(nc.vector.tensor_tensor(ln, ln, m, ALU.add))
            link(nc.vector.tensor_tensor(ln, ln, e, ALU.mult))
            link(nc.vector.tensor_tensor(ln, ln, r, ALU.mult))
            link(nc.vector.scalar_tensor_tensor(ln, z, 0.0, ln, ALU.max, ALU.add))

        def gates_dve1(dve):
            z, az, e, u, ln, d, m, r = (t[:] for t in sp)
            ps = aux[3][:, 0:256].rearrange("p (t two n) -> p t two n", t=TT, two=2)
            nc.vector.tensor_tensor(small[:], ps[:, :, 0], small[:], ALU.add).then_inc(fg_tmp, 1)
            dve.wait_ge(fg_tmp, 4)
            nc.vector.tensor_tensor(small[:], small[:], rstd_c[:].unsqueeze(2).to_broadcast([P, TT, 64]), ALU.mult)\
                .then_inc(gg_dve, 1)
            dve.wait_ge(gg_dve, 1)
            steps = [SPD + 1]

            def link(ins):
                steps[0] += 1
                ins.then_inc(sp_dve, 1)
                dve.wait_ge(sp_dve, steps[0])

            def w2(t):
                return t.rearrange("p (t h) -> p t h", t=TT)

            def both(t):
                return t.unsqueeze(1).to_broadcast([P, TT, V_HEADS])
            link(nc.vector.tensor_tensor(w2(z), small[:, :, 32:64], both(bias[:, 40:72]), ALU.add))
            softplus_steps(dve, link, z, az, e, u, ln, d, m, r, 1, None, None)
            dve.wait_ge(gg_act, 2)
            nc.vector.scalar_tensor_tensor(gate_g[:], w2(ln), -1.0, both(small[:, 0, 0:32]), ALU.mult, ALU.mult)\
                .then_inc(gg_dve, 1)

        def gates_dve2(dve):
            dve.wait_ge(gg_act, 4)
            nc.vector.tensor_tensor(gate_bg[:], gate_b[:], gate_ec[:], ALU.mult).then_inc(gg_dve, 1)
            dve.wait_ge(gg_pe, 2)
            nc.vector.tensor_tensor(gate_ed[:], aux[2][:, 0:64].rearrange("p (t h) -> p t h", t=TT), gate_c[:],
                                    ALU.subtract).then_inc(gg_dve, 1)

        def conv_tap(eng, q, tiles, base):
            k, ct = q // tiles, base + q % tiles
            w = conv_w[:, k, ct:ct + 1]
            if k == 0:
                return eng.tensor_scalar(conv[:, ct], u_pad[:, ct, 0:T], w, vec[:, CB + ct:CB + ct + 1],
                                         ALU.mult, ALU.add)
            return eng.scalar_tensor_tensor(conv[:, ct], u_pad[:, ct, k:k + T], w, conv[:, ct], ALU.mult, ALU.add)

        def conv_taps_dve(dve, n):
            if n < 0:
                return
            if n == 0:
                dve.wait_ge(glu_made, 2)
                for ct in range(CONV_DVE, CT):
                    last = conv_tap(nc.vector, ct - CONV_DVE, CT, CONV_DVE)
                last.then_inc(conv_start, 1)
            for q in range(6 * n, min(6 * n + 6, CONV_W * CONV_DVE)):
                if q >= CONV_DVE:
                    dve.wait_ge(conv_step, q - CONV_DVE + 1)
                conv_tap(nc.vector, q, CONV_DVE, 0).then_inc(conv_step, 1)

        def conv_taps_act(act, n):
            if n == 0:
                act.wait_ge(glu_made, 2)
            for k in range(2 * n + 1, min(2 * n + 3, CONV_W)) if n >= 0 else ():
                if k > 2:
                    act.wait_ge(conv_pool, k - 2)
                for m in range(CT - CONV_DVE):
                    ct = CONV_DVE + m
                    last = nc.scalar.activation(prod[:, k % 2, m], u_pad[:, ct, k:k + T], ACT.Copy,
                                                scale=conv_w[:, k, ct:ct + 1])
                last.then_inc(conv_act, 1)

        def conv_taps_pool(pool):
            pool.wait_ge(conv_start, 1)
            for k in range(1, CONV_W):
                pool.wait_ge(conv_act, k)
                if k > 1:
                    pool.wait_ge(conv_pool, k - 1)
                nc.gpsimd.tensor_tensor(conv[:, CONV_DVE:], conv[:, CONV_DVE:], prod[:, k % 2], ALU.add)\
                    .then_inc(conv_pool, 1)

        def ln_dve_steps(dve):
            dve.wait_ge(conv_step, CONV_W * CONV_DVE)
            dve.wait_ge(conv_pool, CONV_W - 1)
            dve.wait_ge(ln_pe, 1)
            mean = aux[0][:, 0:T].unsqueeze(1).to_broadcast([P, CT, T])
            nc.vector.scalar_tensor_tensor(conv[:], mean, -1.0 / 1024, conv[:], ALU.mult, ALU.add).then_inc(ln_dve, 1)
            dve.wait_ge(ln_act, 2)
            nc.vector.reciprocal(rstd[:], rms[:]).then_inc(ln_dve, 1)
            dve.wait_ge(ln_dve, 2)
            nc.vector.tensor_tensor(conv[:], conv[:], rstd[:].unsqueeze(1).to_broadcast([P, CT, T]), ALU.mult)\
                .then_inc(ln_dve, 1)
        def fox_dve(dve):
            fox_scores(dve, 0)
            fox_max(dve, 0)
            dve.wait_ge(ln_act, 4)
            nc.vector.tensor_tensor(hs[0][:, 8:16, 1, :], u_sq[:], hs[0][:, 8:16, 0, :].bitcast(F32), ALU.subtract)\
                .then_inc(ln_dve, 1)
            for n in range(HEADS0 // 2):
                for p in range(2):
                    dve.wait_ge(fx_act[p], 4 * n + 2)
                    nc.vector.reciprocal(rinv[:, p], rsum[:, p]).then_inc(fx_dve[p], 1)
                for p in range(2):
                    dve.wait_ge(fx_dve[p], FOX_MAX(n) + 1)
                    for t in range(TT):
                        w = sc[:, p, t, 0:P * (t + 1)]
                        last = nc.vector.tensor_scalar(w, w, rinv[:, p, t:t + 1], None, ALU.mult)
                    last.then_inc(fx_dve[p], 1)
                if n < HEADS0 // 2 - 1:
                    fox_scores(dve, n + 1)
                for p in range(2):
                    dve.wait_ge(fx_act[p], 4 * n + 4)
                    nc.vector.tensor_tensor(hs[0][:, 2 * n + p, 1, :], aux[2 * p + 1][:, 0:T],
                                            hs[0][:, 2 * n + p, 0, :].bitcast(F32), ALU.subtract).then_inc(fx_dve[p], 1)
                if n < HEADS0 // 2 - 1:
                    fox_max(dve, n + 1)

        def fox_scores(dve, n):
            for p in range(2):
                h = 2 * n + p
                dve.wait_ge(fx_pe[p], FOX_S(n))
                dve.wait_ge(fox_cp, 2)
                for t in range(TT):
                    last = nc.vector.tensor_scalar(sc[:, p, t, 0:P * (t + 1)], aux[2 * p][:, P * t:P * t + P * (t + 1)],
                                                   1.0 / math.sqrt(P), cq[:, t, h:h + 1], ALU.mult, ALU.add)
                last.then_inc(fx_dve[p], 1)

        def fox_max(dve, n):
            for p in range(2):
                dve.wait_ge(fx_pool[p], n + 1)
                for t in range(TT):
                    last = nc.vector.tensor_reduce(mx[:, p, t:t + 1], sc[:, p, t, 0:P * (t + 1)], AX.X, ALU.max,
                                                   negate=True)
                last.then_inc(fx_dve[p], 1)

        def gdn_dve(dve, j):
            dve.wait_ge(gg_act, 6)
            for _ in range(PRELUDE - 4):
                yield
            for h in range(2):
                dve.wait_ge(l2_act, 6 * j + 6)
                nc.vector.tensor_tensor(qk[:, h], qk_in[:, h], qk_sq[:, h], ALU.mult).then_inc(l2_dve, 1)
                yield
            yield
            yield
            for u in range(2):
                yield from gdn_dve_steps(dve, j, u)

        def pairs(t, j, a):
            v = t[:, :, bass.ds(SV * j + 2 * a, 2)].rearrange("p t b -> p b t")
            return v.unsqueeze(3).to_broadcast([P, 2, TT, P])

        def four(t):
            return t.rearrange("p (b t) i -> p b t i", b=2)

        def bank(p, w):
            return aux[2 * p + w][:].rearrange("p (b t i) -> p b t i", b=2, t=TT)

        def over_b(t):
            return t.unsqueeze(1).to_broadcast([P, 2, TT, P])

        def gdn_dve_steps(dve, j, u):
            n = 2 * j + u
            ident4 = ident[:].unsqueeze(1).to_broadcast([P, 4, P])
            for p in range(2):
                dve.wait_ge(gd_pe[p], NP * n + P_GB)
                nc.vector.tensor_tensor(four(slot[p][0][:]), pairs(gate_c, j, 2 * u + p), bank(p, 0), ALU.subtract)\
                    .then_inc(gd_dve[p], 1)
                yield
            yield from rest(j, 2)
            for p in range(2):
                dve.wait_ge(gd_pe[p], NP * n + P_KK)
                dve.wait_ge(gd_act[p], NA * n + A_DECAY)
                kk = aux[2 * p + 1][:, 0:256].rearrange("p (t i) -> p t i", t=TT)
                qq = aux[2 * p + 1][:, 256:512].rearrange("p (t i) -> p t i", t=TT)
                nc.vector.tensor_tensor(four(slot[p][1][:]), over_b(kk), four(slot[p][0][:]), ALU.mult)\
                    .then_inc(gd_dve[p], 1)
                nc.vector.tensor_tensor(four(slot[p][2][:]), over_b(qq), four(slot[p][0][:]), ALU.mult)\
                    .then_inc(gd_dve[p], 1)
                yield
            yield from rest(j, 2)
            for p in range(2):
                dve.wait_ge(gd_pool[p], NO * n + O_R1)
                nc.vector.tensor_tensor(slot[p][5][:], ident4, slot[p][5][:], ALU.subtract).then_inc(gd_dve[p], 1)
                yield
            for p in range(2):
                dve.wait_ge(gd_pool[p], NO * n + O_Q1)
                nc.vector.tensor_tensor(slot[p][6][:], ident4, slot[p][6][:], ALU.subtract).then_inc(gd_dve[p], 1)
                yield
            for lv in range(1, LEVELS):
                yield
                yield
                for p in range(2):
                    dve.wait_ge(gd_pe[p], NP * n + P_LV(lv, 1))
                    w = slot[p][5] if lv < LEVELS - 1 else slot[p][6]
                    nc.vector.tensor_tensor(flat(w[:]), flat(w[:]), aux[2 * p + 1][:], ALU.subtract)\
                        .then_inc(gd_dve[p], 1)
                    yield
                if lv < LEVELS - 1:
                    yield
                    yield
            for p in range(2):
                a = 2 * u + p
                dve.wait_ge(gd_pe[p], NP * n + P_KT)
                kt = aux[2 * p][:, 0:256].rearrange("p (t i) -> p t i", t=TT)
                nc.vector.tensor_tensor(four(slot[p][1][:]), over_b(kt), pairs(gate_bg, j, a), ALU.mult)\
                    .then_inc(gd_dve[p], 1)
                nc.vector.tensor_tensor(four(slot[p][2][:]), over_b(kt), pairs(gate_ed, j, a), ALU.mult)\
                    .then_inc(gd_dve[p], 1)
                nc.vector.tensor_tensor(four(slot[p][0][:]), bank(p, 1), pairs(gate_b, j, a), ALU.mult)\
                    .then_inc(gd_dve[p], 1)
                yield
            yield
            yield
            for c in range(4):
                t, r = c // 2, slice(64 * (c % 2), 64 * (c % 2) + 64)
                for p in range(2):
                    if c:
                        dve.wait_ge(gd_pe[p], NP * n + P_WS(c))
                        dve.wait_ge(gd_act[p], NA * n + A_U)
                        v = four(slot[p][4][:])[r, :, t, :]
                        nc.vector.tensor_tensor(v, v, aux[2 * p][r, 0:256].rearrange("p (b i) -> p b i", b=2),
                                                ALU.subtract).then_inc(gd_dve[p], 1)
                        yield
                if c < 3:
                    for p in range(2):
                        a = 2 * u + p
                        dve.wait_ge(gd_pe[p], NP * n + P_DS(c))
                        for b in range(2):
                            ds_ = aux[2 * p + 1][:, b * P:(b + 1) * P]
                            if c == 0:
                                i_ = nc.vector.tensor_copy(state[p][:, b], ds_)
                            else:
                                i_ = nc.vector.scalar_tensor_tensor(
                                    state[p][:, b], state[p][:, b], gate_el[:, c, bass.ds(SV * j + 2 * a + b, 1)],
                                    ds_, ALU.mult, ALU.add)
                        i_.then_inc(gd_dve[p], 1)
                        yield
            for p in range(2):
                dve.wait_ge(gd_pe[p], NP * n + P_O)
                dve.wait_ge(gd_act[p], NA * n + A_QS)
                dve.wait_ge(gd_pool[p], NO * n + O_ZERO)
                nc.vector.tensor_tensor(flat(slot[p][0][:]), aux[2 * p][:], flat(slot[p][1][:]), ALU.add)\
                    .then_inc(gd_dve[p], 1)
                yield
            yield from rest(j, 1)
            for p in range(2):
                dve.wait_ge(gd_pool[p], NO * n + O_SQ)
                nc.vector.tensor_reduce(o_ss[:, p], slot[p][1][:], AX.X, ALU.add).then_inc(gd_dve[p], 1)
                dve.wait_ge(gd_act[p], NA * n + A_RMS)
                nc.vector.reciprocal(o_rs[:, p], o_rs[:, p]).then_inc(gd_dve[p], 1)
                yield
            yield from rest(j, 1)
            for p in range(2):
                a = 2 * u + p
                dve.wait_ge(gd_pe[p], NP * n + P_OT)
                nc.vector.scalar_tensor_tensor(
                    og[:, 2 * a:2 * a + 2, :].rearrange("p b t -> p (b t)"), aux[2 * p + 1][:],
                    vec[:, ON:ON + 1], zs[:, 2 * a:2 * a + 2, :].rearrange("p b t -> p (b t)"), ALU.mult, ALU.mult)\
                    .then_inc(gd_dve[p], 1)
                yield

        def gdn_pool(pool, j):
            pool.wait_ge(gg_dve, 4)
            pool.wait_ge(gg_act, 6)
            nc.gpsimd.tensor_copy(g_set[:], gate_g[:, :, bass.ds(SV * j, SV)]).then_inc(gset_ready, 1)
            for _ in range(PRELUDE):
                yield
            for u in range(2):
                yield from gdn_pool_steps(pool, j, u)
            for p in range(2):
                pool.wait_ge(gd_dve[p], ND * (2 * j + 2))
            apart(pool)
            pool.dma_start(og_rows(j), og[:]).then_inc(og_saved, 16)
            pool.wait_ge(og_saved, 16 * j + 16)

        def gdn_pool_steps(pool, j, u):
            n = 2 * j + u

            def mask4(m):
                return m.unsqueeze(1).to_broadcast([P, 4, P])
            def level_mask(p, lv):
                if lv == 1:
                    pool.wait_ge(gd_dve[p], ND * n + D_QK)
                elif lv == 2:
                    pool.wait_ge(gd_pe[p], NP * n + P_LT)
                    pool.wait_ge(gd_pool[p], NO * n + O_R1)
                else:
                    pool.wait_ge(gd_pe[p], NP * n + P_LV(lv - 2, 0))
                nc.gpsimd.tensor_tensor(slot[p][(lv + 1) % 2][:], slot[p][4][:], mask4(lvl[:, lv, :]), ALU.mult)\
                    .then_inc(gd_pool[p], 1)

            for p in range(2):
                pool.wait_ge(gd_dve[p], ND * n + D_DIFF)
                s0 = slot[p][0]
                nc.gpsimd.tensor_tensor(s0[:], s0[:], mask4(mask_gdn[:]), ALU.add).then_inc(gd_pool[p], 1)
                yield
            for p in range(2):
                a = 2 * u + p
                pool.wait_ge(gd_dve[p], ND * n + D_KK)
                apart(pool)
                s1 = four(slot[p][1][:])
                nc.gpsimd.tensor_tensor(s1, s1, pairs(gate_b, j, a), ALU.mult).then_inc(gd_pool[p], 1)
                yield
            yield from rest(j, 4)
            for p in range(2):
                pool.wait_ge(gd_pool[p], NO * n + O_BETA)
                nc.gpsimd.tensor_tensor(slot[p][5][:], slot[p][1][:], mask4(lvl0t[:]), ALU.mult)\
                    .then_inc(gd_pool[p], 1)
                yield
            for p in range(2):
                pool.wait_ge(gd_act[p], NA * n + A_LT)
                nc.gpsimd.tensor_tensor(slot[p][6][:], slot[p][4][:], mask4(lvl[:, 0, :]), ALU.mult)\
                    .then_inc(gd_pool[p], 1)
                level_mask(p, 1)
                yield
            for lv in range(1, LEVELS):
                for p in range(2):
                    if lv < LEVELS - 1:
                        level_mask(p, lv + 1)
                    yield
                for _ in range(4 if lv < LEVELS - 1 else 2):
                    yield
            yield
            yield
            for p in range(2):
                pool.wait_ge(gd_pe[p], NP * n + P_W)
                apart(pool)
                pool.memset(four(slot[p][1][:])[0:64, :, 0, :], 0.0).then_inc(gd_pool[p], 1)
                yield
            for _ in range(12):
                yield
            for p in range(2):
                pool.wait_ge(gd_dve[p], ND * n + D_O)
                nc.gpsimd.tensor_tensor(slot[p][1][:], slot[p][0][:], slot[p][0][:], ALU.mult)\
                    .then_inc(gd_pool[p], 1)
                yield
            for p in range(2):
                pool.wait_ge(gd_dve[p], ND * n + D_RS)
                rs = o_rs[:, p].unsqueeze(2).to_broadcast([P, 4, P])
                nc.gpsimd.tensor_tensor(slot[p][0][:], slot[p][0][:], rs, ALU.mult).then_inc(gd_pool[p], 1)
                yield
            yield
            yield
            yield from rest(j, 2)

        def fox_pool(pool):
            for h in range(HEADS0):
                p, n = h % 2, h // 2
                pool.wait_ge(fx_dve[p], FOX_SCALED(n))
                for t in range(TT):
                    w = sc[:, p, t, P * t:P * (t + 1)]
                    last = nc.gpsimd.tensor_tensor(w, w, mask_fox[:], ALU.add)
                last.then_inc(fx_pool[p], 1)

        def tensor_program(pe):
            mm, tr = nc.tensor.matmul, nc.tensor.transpose

            pe.wait_ge(const_in, 16 * 15)
            pe.wait_ge(const_step, N_CONST_PE)
            tr(aux[0][:, 0:NVEC], vrow[0:NVEC, 0, :], ident[0:NVEC, 0:NVEC]).then_inc(const_pe, 1)
            tr(aux[1][:, 0:124], vrow[0:124, 1, :], ident[0:124, 0:124]).then_inc(const_pe, 1)
            tr(aux[1][:, 124:248], vrow[0:124, 2, :], ident[0:124, 0:124]).then_inc(const_pe, 1)
            tr(aux[2][:, 0:128], vrow[:, 3, :], ident[:]).then_inc(const_pe, 1)
            tr(aux[2][:, 128:256], vrow[:, 4, :], ident[:]).then_inc(const_pe, 1)
            mm(aux[3][:, 0:72], ones[0:1, :], brow[:], start=True, stop=True).then_inc(const_pe, 1)
            pe.wait_ge(x_in, 16)
            for k in range(0, KT, 2):
                if k >= 8:
                    pe.wait_ge(x_copied, k - 6)
                for h in range(2):
                    for t in range(TT):
                        last = tr(acc[:, (k // 2) % 4, h * T + t * P:h * T + (t + 1) * P],
                                  stage[:, t, (k + h) * P:(k + h + 1) * P], ident[:])
                last.then_inc(x_trans, 1)

            def norm(n):
                pe.wait_ge(sq_added, 16 * n + 16)
                mm(aux[0][:, 0:T], ones[:], sq_acc[:], start=True, stop=True)
                for t in range(TT):
                    last = mm(aux[0][:, T + t:T + t + 1], sq_acc[:, t * P:(t + 1) * P], ones[:, 0:1], start=True, stop=True)
                last.then_inc(ss_ready, 1)

            def narrow(which, n):
                pe.wait_ge(wsm_lo, which + 1)
                for t in range(TT):
                    o = aux[3][:, 2 * n * t:2 * n * (t + 1)]
                    for k in range(KT):
                        fr = slice(t * P, (t + 1) * P)
                        mm(o, xs[:, k, 0, fr], wsm_s[:, k, 0:2 * n], start=k == 0, stop=k == KT - 1,
                           skip_group_check=True)
                        last = mm(o[:, 0:n], xs[:, k, 1, fr], wsm_s[:, k, 0:n], start=False, stop=k == KT - 1,
                                  skip_group_check=True)
                last.then_inc(wsm_mm, 1)

            pe.wait_ge(const_step, N_CONST)
            pe.wait_ge(const_cp, 4)
            steps = [iter(())]

            def visit(here, before, kc_):
                s, i, b, g, G = here.s, here.i, here.b, here.g, here.G
                r = rhs_of(g)
                if s.name == "out0" and here.starts:
                    pe.wait_ge(conv_step, CONV_W * CONV_DVE)
                    pe.wait_ge(conv_pool, CONV_W - 1)
                    for c in range(CT):
                        last = mm(aux[0][:, 0:T], ones[:], conv[:, c], start=c == 0, stop=c == CT - 1)
                    last.then_inc(ln_pe, 1)
                    fox_values_pe(pe, tr, s)
                    pe.wait_ge(ln_act, 1)
                    for c in range(CT):
                        last = mm(aux[1][:, 0:T], ones[:], u_sq[:, c], start=c == 0, stop=c == CT - 1)
                    last.then_inc(ln_pe, 1)
                    fox_pe_steps(pe, mm, tr)
                if s.deltanet and b == 0:
                    steps[0] = gdn_pe(pe, mm, tr, set_of(here))
                for c in range(NCH):
                    pe.wait_ge(lo_ready, 8 * G + 2 * c + 2)
                    if s.name in NORMED and here.starts:
                        pe.wait_ge(xs_ready, 4 * g.norm + c + 1)
                    if s.name == "in1_last" and b == 2:
                        pe.wait_ge(og_ready, c + 1)
                    if s.name == "out1b":
                        pe.wait_ge(og_ready, 4 + c + 1)
                    if s.name.startswith("down"):
                        pe.wait_ge(h_ready, DOWN_NEEDS(s, g))
                    if s.name == "out0" and c == 0:
                        pe.wait_ge(ln_dve, 4)
                        for p in range(2):
                            pe.wait_ge(fx_dve[p], 5 * HEADS0 // 2)
                    for m in range(GM):
                        if c == 0:
                            if is_first(G):
                                pe.wait_ge(x_copied, KT)
                            else:
                                pe.wait_ge(acc_free, 4 * G + m - 3)
                        for k in range(g.kc):
                            kk = g.kc * c + k
                            end = kk == NCH * g.kc - 1
                            cols = slice(m * P, (m + 1) * P)
                            mm(acc[:, m, :], w_hi[:, c % 2, k, cols], r[:, kk], start=kk == 0, stop=end,
                               skip_group_check=True)
                            last = mm(acc[:, m, T:2 * T], w_lo[:, c % 2, k, cols], r[:, kk, 0], start=False,
                                      stop=end, skip_group_check=True)
                            if k == g.kc - 1:
                                if c == NCH - 1:
                                    last.then_inc(acc_ready, 1)
                                elif m == GM - 1:
                                    last.then_inc(w_used, 1)
                            if s.deltanet and 4 * m + k in (2, 5, 7, 10, 12, 15):
                                tick(steps)
                    if s.name in NORMED and here.starts and c == 1:
                        norm(g.norm)
                n = G - s.first
                if s.name == "glu" and n == 0:
                    narrow(0, HEADS0)
                if s.name == "glu" and n == 1:
                    pe.wait_ge(fox_lf, 1)
                    for t in range(TT):
                        o = aux[2][:, 8 * t:8 * t + 8]
                        for q in range(t + 1):
                            w = triu if q == t else ones
                            mm(o, w[:], logf[:, q], start=q == 0, stop=q == t)
                    for t in range(TT):
                        o2 = aux[1][0:HEADS0, t * P:(t + 1) * P]
                        for q in range(t + 1):
                            w = triu if q == t else ones
                            last = mm(o2, logf[:, q], w[:], start=q == 0, stop=q == t)
                    last.then_inc(fox_pe0, 1)
                if s.name == "in1_first" and n == 0:
                    narrow(1, 64)
                if s.name == "in1_first" and n == 1:
                    pe.wait_ge(gg_dve, 2)
                    for t in range(TT):
                        mm(aux[1][:, 32 * t:32 * t + 32], chunk_triu[:], gate_g[:, t], start=True, stop=True)
                    for t in range(TT):
                        last = mm(aux[2][:, 32 * t:32 * t + 32], chunk_ones[:], gate_g[:, t], start=True, stop=True)
                    last.then_inc(gg_pe, 1)
                    for c in range(4):
                        mine = chunk_ones[:, 64 * (c % 2):64 * (c % 2) + 1].to_broadcast([P, P])
                        last = mm(aux[3][:, 32 * c:32 * c + 32], mine, gate_g[:, c // 2], start=True, stop=True)
                    last.then_inc(gg_pe, 1)
                if s.deltanet and b == len(s.groups) - 1:
                    for _ in steps[0]:
                        pass
            walk(pe, visit)
            norm(4)
            for k in range(KT // 2):
                pe.wait_ge(y_made, k // 2 + 1)
                if k >= 2:
                    pe.wait_ge(y_out, 2 * k - 2)
                for t in range(TT):
                    for h in range(2):
                        last = tr(aux[(2 * k + t) % 4][:, h * P:(h + 1) * P], xT[:, 2 * k + h, t * P:(t + 1) * P], ident[:])
                last.then_inc(y_pe, 1)

        def DOWN_NEEDS(s, g):
            layer_pairs = 0 if s.resid < 16 else 11
            return layer_pairs + min(11, 4 * (g.at + 1))

        def fox_values_pe(pe, tr, s):
            pe.wait_ge(scaled, s.scaled)
            pe.wait_ge(fox_cp, 2)
            for h in range(HEADS0):
                if h >= 2:
                    pe.wait_ge(vt_act, h - 1)
                for t in range(TT):
                    last = tr(aux[2 + h % 2][:, t * P:(t + 1) * P], vT[:, h, t * P:(t + 1) * P], ident[:])
                last.then_inc(vt_pe, 1)

        def fox_pe_steps(pe, mm, tr):
            def scores(n):
                for p in range(2):
                    h = 2 * n + p
                    sel = ident[0:HEADS0, h:h + 1].to_broadcast([HEADS0, P])
                    for t in range(TT):
                        o = aux[2 * p][:, P * t:P * t + P * (t + 1)]
                        mm(o, qT[:, h, t * P:(t + 1) * P], kT[:, h, 0:P * (t + 1)], start=True, stop=False)
                        last = mm(o, sel, ncT[:, 0:P * (t + 1)], start=False, stop=True)
                    last.then_inc(fx_pe[p], 1)
            pe.wait_ge(vt_act, HEADS0)
            scores(0)
            for n in range(HEADS0 // 2):
                for p in range(2):
                    B = aux[2 * p + 1]
                    pe.wait_ge(fx_dve[p], FOX_MAX(n) + 2)
                    if n == 0:
                        pe.wait_ge(ln_act, 2)
                    tr(B[:, 0:P], sc[:, p, 0, 0:P], ident[:])
                    for q in range(TT):
                        last = tr(B[:, P * (q + 1):P * (q + 2)], sc[:, p, 1, q * P:(q + 1) * P], ident[:])
                    last.then_inc(fx_pe[p], 1)
                if n < HEADS0 // 2 - 1:
                    scores(n + 1)
                for p in range(2):
                    B, h = aux[2 * p + 1], 2 * n + p
                    pe.wait_ge(fx_act[p], 4 * n + 3)
                    mm(B[:, 0:T], v_tok[:, h, 0], pT[:, p, 0:T], start=True, stop=False, skip_group_check=True)
                    mm(B[:, P:T], v_tok[:, h, 1], pT[:, p, T:T + P], start=False, stop=True, skip_group_check=True)\
                        .then_inc(fx_pe[p], 1)

        def gdn_pe(pe, mm, tr, j):
            for _ in range(4):
                yield
            pe.wait_ge(l2_act, 6 * j + 1)
            for n in range(2):
                mm(aux[n][:], ones[:], qk_sq[:, n // 2, 2 * (n % 2):2 * (n % 2) + 2, :], start=True, stop=True)
            yield
            for n in range(2, 4):
                last = mm(aux[n][:], ones[:], qk_sq[:, n // 2, 2 * (n % 2):2 * (n % 2) + 2, :], start=True, stop=True)
            last.then_inc(l2_pe, 1)
            for _ in range(PRELUDE - 5):
                yield
            pe.wait_ge(gset_ready, j + 1)
            pe.wait_ge(l2_dve, 2 * j + 2)
            for u in range(2):
                yield from gdn_pe_steps(pe, mm, tr, j, u)

        def gdn_pe_steps(pe, mm, tr, j, u):
            n = 2 * j + u

            def fr(t):
                return slice(t * P, (t + 1) * P)
            for p in range(2):
                a = 2 * u + p
                A, B = aux[2 * p], aux[2 * p + 1]
                if u:
                    pe.wait_ge(gd_dve[p], ND * n)
                for b in range(2):
                    for t in range(TT):
                        g = g_set[:, t, 2 * a + b:2 * a + b + 1].to_broadcast([P, P])
                        last = mm(A[:, fr(2 * b + t)], g, chunk_triu[:], start=True, stop=True)
                last.then_inc(gd_pe[p], 1)
                for t in range(TT):
                    mm(B[:, fr(t)], qk[:, 1, a, fr(t)], qk[:, 1, a, fr(t)], start=True, stop=True)
                for t in range(TT):
                    last = mm(B[:, fr(2 + t)], qk[:, 0, a, fr(t)], qk[:, 1, a, fr(t)], start=True, stop=True)
                last.then_inc(gd_pe[p], 1)
                yield
            yield
            yield
            yield from rest(j, 4)
            for p in range(2):
                A, B = aux[2 * p], aux[2 * p + 1]
                pe.wait_ge(gd_pool[p], NO * n + O_BETA)
                for q in range(4):
                    last = tr(A[:, fr(q)], slot[p][1][:, q], ident[:])
                last.then_inc(gd_pe[p], 1)
                pe.wait_ge(gd_dve[p], ND * n + D_QK)
                for q in range(4):
                    last = tr(B[:, fr(q)], slot[p][2][:, q], ident[:])
                last.then_inc(gd_pe[p], 1)
                yield
            yield
            yield
            for lv in range(1, LEVELS):
                for p in range(2):
                    pe.wait_ge(gd_pool[p], NO * n + O_M(lv))
                    pe.wait_ge(gd_dve[p], ND * n + (D_Q1 if lv == 1 else D_LV(lv - 1)))
                    if lv > 1:
                        pe.wait_ge(gd_act[p], NA * n + A_LV(lv - 1, 1))
                    else:
                        pe.wait_ge(gd_act[p], NA * n + A_IT)
                    for q in range(4):
                        last = mm(aux[2 * p][:, fr(q)], slot[p][(lv + 1) % 2][:, q], slot[p][5][:, q], start=True, stop=True)
                    last.then_inc(gd_pe[p], 1)
                    yield
                for p in range(2):
                    pe.wait_ge(gd_act[p], NA * n + A_LV(lv, 0))
                    for q in range(4):
                        w, r = (slot[p][6], slot[p][2]) if lv < LEVELS - 1 else (slot[p][2], slot[p][6])
                        last = mm(aux[2 * p + 1][:, fr(q)], w[:, q], r[:, q], start=True, stop=True)
                    last.then_inc(gd_pe[p], 1)
                    yield
                if lv < LEVELS - 1:
                    for p in range(2):
                        pe.wait_ge(gd_dve[p], ND * n + D_LV(lv))
                        for q in range(4):
                            last = tr(aux[2 * p][:, fr(q)], slot[p][5][:, q], ident[:])
                        last.then_inc(gd_pe[p], 1)
                        yield
            for p in range(2):
                a = 2 * u + p
                A, B = aux[2 * p], aux[2 * p + 1]
                for t in range(TT):
                    last = tr(A[:, fr(t)], qk[:, 1, a, fr(t)], ident[:])
                pe.wait_ge(gd_dve[p], ND * n + D_LV(LEVELS - 1))
                for b in range(2):
                    for t in range(TT):
                        last = tr(B[:, fr(2 * b + t)], vs[:, 2 * a + b, fr(t)], ident[:])
                last.then_inc(gd_pe[p], 1)
                yield
            for p in range(2):
                A, B = aux[2 * p], aux[2 * p + 1]
                pe.wait_ge(gd_dve[p], ND * n + D_VB)
                for q in range(4):
                    last = mm(A[:, fr(q)], slot[p][6][:, q], slot[p][0][:, q], start=True, stop=True)
                last.then_inc(gd_pe[p], 1)
                for q in range(4):
                    last = mm(B[:, fr(q)], slot[p][1][:, q], slot[p][6][:, q], start=True, stop=True)
                last.then_inc(gd_pe[p], 1)
                yield
            for c in range(4):
                t, r = c // 2, slice(64 * (c % 2), 64 * (c % 2) + 64)
                if c:
                    for p in range(2):
                        a = 2 * u + p
                        A = aux[2 * p]
                        pe.wait_ge(gd_dve[p], ND * n + D_S(c - 1))
                        pe.wait_ge(gd_act[p], NA * n + (A_W if c == 1 else A_QC(c - 1)))
                        for b in range(2):
                            mm(A[:, fr(b)], slot[p][5][:, 2 * b + t], state[p][:, b], start=True, stop=True)
                        mm(A[:, T:2 * T], qk[:, 0, a, fr(t)], state[p][:], start=True, stop=True)\
                            .then_inc(gd_pe[p], 1)
                        yield
                if c < 3:
                    for p in range(2):
                        B = aux[2 * p + 1]
                        if c:
                            pe.wait_ge(gd_dve[p], ND * n + D_VN(c))
                        else:
                            pe.wait_ge(gd_act[p], NA * n + A_W)
                        for b in range(2):
                            last = mm(B[:, fr(b)], slot[p][2][r, 2 * b + t], slot[p][4][r, 2 * b + t], start=True, stop=True)
                        last.then_inc(gd_pe[p], 1)
                        yield
            for p in range(2):
                pe.wait_ge(gd_dve[p], ND * n + D_VN(3))
                pe.wait_ge(gd_act[p], NA * n + A_QS)
                for q in range(4):
                    last = mm(aux[2 * p][:, fr(q)], slot[p][3][:, q], slot[p][4][:, q], start=True, stop=True)
                last.then_inc(gd_pe[p], 1)
                yield
            yield
            yield
            yield from rest(j, 2)
            for p in range(2):
                pe.wait_ge(gd_pool[p], NO * n + O_ON)
                for q in range(4):
                    last = tr(aux[2 * p + 1][:, fr(q)], slot[p][0][:, q], ident[:])
                last.then_inc(gd_pe[p], 1)
                yield


        block = ctx.enter_context(nc.Block())

        @block.sync
        def _(eng):
            sync_program(eng)

        @block.gpsimd
        def _(eng):
            pool_program(eng)

        @block.scalar
        def _(eng):
            scalar_program(eng)

        @block.vector
        def _(eng):
            vector_program(eng)

        @block.tensor
        def _(eng):
            tensor_program(eng)


NORMED = ("glu", "gu0", "in1_first")
K_SILU = 2

CONV_DVE = 4


def FOX_S(n):
    return 3 * n if n else 1


def FOX_TR(n):
    return 3 * n + 2


def FOX_AV(n):
    return min(3 * n + 4, 3 * HEADS0 // 2)


def FOX_SCALED(n):
    return 5 * n if n else 1


def FOX_MAX(n):
    return 5 * n + 2


PRELUDE = 16

SPD = 12
N_CONST = 40
N_CONST_PE = 3

P_GB, P_KK, P_LT, P_IT = 1, 2, 3, 4


def P_LV(lv, k):
    return 4 + 3 * (lv - 1) + k + 1


P_KT = P_LV(LEVELS - 1, 1) + 1
P_U, P_W = P_KT + 1, P_KT + 2


def P_DS(c):
    return P_W + 1 + 2 * c


def P_WS(c):
    return P_W + 2 * c


P_O = P_WS(3) + 1
P_OT = P_O + 1
NP = P_OT

A_DECAY, A_LT, A_IT = 1, 2, 3


def A_LV(lv, k):
    return 3 + 2 * (lv - 1) + k + 1


A_U = A_LV(LEVELS - 1, 0) + 1
A_W = A_U + 1


def A_QC(c):
    return A_W + 2 * c


A_QS = A_QC(3)
A_RMS = A_QS + 1
NA = A_RMS

D_DIFF, D_KK, D_QK, D_R1, D_Q1 = 1, 2, 3, 4, 5


def D_LV(lv):
    return 5 + lv


D_KBG, D_KDEC, D_VB = (D_LV(LEVELS - 1) + n for n in (1, 2, 3))


def D_S(c):
    return D_VB + 1 + 2 * c


def D_VN(c):
    return D_VB + 2 * c


D_O = D_VN(3) + 1
D_SS, D_RS, D_OG = D_O + 1, D_O + 2, D_O + 3
ND = D_OG

O_MASK, O_BETA, O_R1, O_Q1 = 1, 2, 3, 4


def O_M(lv):
    return 4 + lv


O_ZERO = O_M(LEVELS - 1) + 1
O_SQ, O_ON = O_ZERO + 1, O_ZERO + 2
NO = O_ON

_INS = ["x", "norm_mix0", "w_in0", "fgate_bias0", "conv_w0", "conv_b0", "conv_ln_g0", "conv_ln_b0", "w_out0",
        "norm_mix1", "w_in1", "short_conv1", "a_log1", "dt_bias1", "o_norm1", "w_out1",
        "norm_ffn", "w_gate", "w_up", "w_down", "final_norm"]


def kernel(**inputs):
    import numpy as _np
    import concourse.bacc as _bacc
    from concourse import mybir as _mybir
    from concourse.bass_utils import run_bass_kernel_spmd as _run

    nc = _bacc.Bacc("TRN2", target_bir_lowering=False, num_devices=1)
    arrays, args = {}, []
    for name in _INS:
        a = _np.ascontiguousarray(inputs[name])
        arrays[f"in_{name}"] = a
        args.append(nc.dram_tensor(f"in_{name}", a.shape, _mybir.dt.from_np(a.dtype), kind="ExternalInput").ap())
    save = nc.dram_tensor("og_save", (V_HEADS * P, T), _mybir.dt.float32, kind="Internal").ap()
    out = nc.dram_tensor("out", (1, T, D), _mybir.dt.float32, kind="ExternalOutput").ap()
    trunk(nc, *args, save, out)
    r = _run(nc, [arrays], core_ids=[0])
    return r.results[0]["out"]
```
